# Optimizing a Trainium2 kernel written in Bass

```python
import jax, jax.numpy as jnp
from jax import lax
import numpy as np
import math

D_MODEL = 1024
BATCH = 1
SEQ = 512
DEPTH = 1

N_META = 16
POOL_WIDTH = D_MODEL // 2
POOL_WINDOWS = (2, 4, 8, 16)
POOL_GROUP = POOL_WIDTH // len(POOL_WINDOWS)
N_HEADS = 8
HEAD_DIM = 64
ATTN_WIDTH = N_HEADS * HEAD_DIM
Q_BLOCK = 128
RMS_EPS = 1e-6
IN_SIZES = (POOL_WIDTH, POOL_WIDTH, ATTN_WIDTH, ATTN_WIDTH, ATTN_WIDTH, ATTN_WIDTH, N_HEADS, D_MODEL, D_MODEL)
N_IN = 2 * POOL_WIDTH + 4 * ATTN_WIDTH + N_HEADS + 2 * D_MODEL


def _split_points():
    pts, acc = [], 0
    for s in IN_SIZES[:-1]:
        acc += s
        pts.append(acc)
    return pts

def rmsnorm(x, g):
    xf = x.astype(jnp.float32)
    xf = xf * lax.rsqrt(jnp.mean(xf * xf, axis=-1, keepdims=True) + RMS_EPS)
    return (xf * g.astype(jnp.float32)).astype(x.dtype)

def causal_multiscale_pool(u, pool_w, pool_scale):
    B, L, _ = u.shape
    groups = jnp.split(u, len(POOL_WINDOWS), axis=-1)
    pos = jnp.arange(L, dtype=jnp.float32)[:, None]
    pooled = []
    for w, ug in zip(POOL_WINDOWS, groups):
        uf = ug.astype(jnp.float32)
        c = jnp.cumsum(uf, axis=1)
        c_prev = jnp.pad(c, ((0, 0), (w, 0), (0, 0)))[:, :L]
        count = jnp.minimum(pos + 1.0, float(w))
        pooled.append((c - c_prev) / count - uf)
    p = jnp.stack(pooled, axis=2).astype(u.dtype)
    y = jnp.einsum('blgc,gcd->blgd', p, pool_w)
    return y.reshape(B, L, POOL_WIDTH) * pool_scale

def forgetting_attention(q, k, v, log_f):
    B, L, H, Dh = q.shape
    pad = (Q_BLOCK - L % Q_BLOCK) % Q_BLOCK
    padw = ((0, 0), (pad, 0), (0, 0), (0, 0))
    qp, kp, vp = jnp.pad(q, padw), jnp.pad(k, padw), jnp.pad(v, padw)
    c = jnp.cumsum(log_f, axis=1)
    c = jnp.transpose(jnp.pad(c, ((0, 0), (pad, 0), (0, 0))), (0, 2, 1))
    Lp = L + pad
    scale = 1.0 / np.sqrt(HEAD_DIM)
    outs = []
    for i in range(Lp // Q_BLOCK):
        q0, q1 = i * Q_BLOCK, (i + 1) * Q_BLOCK
        qb, kb, vb = qp[:, q0:q1], kp[:, :q1], vp[:, :q1]
        s = jnp.einsum('bqhd,bkhd->bhqk', qb, kb).astype(jnp.float32) * scale
        s = s + c[:, :, q0:q1, None] - c[:, :, None, :q1]
        q_idx = jnp.arange(q0, q1)[:, None]
        k_idx = jnp.arange(q1)[None, :]
        valid = (k_idx <= q_idx) & ((k_idx >= pad) | (k_idx == q_idx))
        s = jnp.where(valid, s, -jnp.inf)
        p = jax.nn.softmax(s, axis=-1)
        outs.append(jnp.einsum('bhqk,bkhd->bqhd', p.astype(vb.dtype), vb))
    o = jnp.concatenate(outs, axis=1)[:, pad:]
    return o

def hybrid_layer(x, norm_g, w_in, b_forget, pool_w, pool_scale, w_up_pool, w_up_attn, w_out):
    B, L, _ = x.shape
    h = rmsnorm(x, norm_g)
    proj = jnp.einsum('bld,dn->bln', h, w_in)
    u_pool, z_pool, q, k, v, z_attn, f_logit, g_pool, g_attn = jnp.split(proj, _split_points(), axis=-1)
    y_pool = causal_multiscale_pool(u_pool, pool_w, pool_scale) * jax.nn.silu(z_pool)
    q = q.reshape(B, L, N_HEADS, HEAD_DIM)
    k = k.reshape(B, L, N_HEADS, HEAD_DIM)
    v = v.reshape(B, L, N_HEADS, HEAD_DIM)
    log_f = jax.nn.log_sigmoid((f_logit + b_forget).astype(jnp.float32))
    y_attn = forgetting_attention(q, k, v, log_f).reshape(B, L, ATTN_WIDTH) * jax.nn.silu(z_attn)
    merged = (jax.nn.sigmoid(g_pool) * jnp.einsum('blc,cd->bld', y_pool, w_up_pool)
              + jax.nn.sigmoid(g_attn) * jnp.einsum('blc,cd->bld', y_attn, w_up_attn))
    return x + jnp.einsum('bld,de->ble', merged, w_out)

def first_inputs(seed: int = 0) -> dict:
    key = jax.random.key(seed)
    ks = jax.random.split(key, 12)
    f0 = sum(IN_SIZES[:6])
    x = jax.random.normal(ks[0], (BATCH, SEQ, D_MODEL), jnp.float32)
    meta_tokens = jax.random.normal(ks[1], (N_META, D_MODEL), jnp.float32)
    norm_g = 1.0 + 0.02 * jax.random.normal(ks[2], (DEPTH, D_MODEL), jnp.float32)
    w_in = jax.random.normal(ks[3], (DEPTH, D_MODEL, N_IN), jnp.float32) * D_MODEL ** -0.5
    w_in = w_in.at[:, :, f0:f0 + N_HEADS].multiply(0.1)
    b_forget = (jnp.linspace(1.0, 6.0, N_HEADS, dtype=jnp.float32)[None, :]
                + 0.1 * jax.random.normal(ks[4], (DEPTH, N_HEADS), jnp.float32))
    pool_w = jax.random.normal(ks[5], (DEPTH, len(POOL_WINDOWS), POOL_GROUP, POOL_GROUP), jnp.float32) * POOL_GROUP ** -0.5
    pool_scale = 1.0 + 0.1 * jax.random.normal(ks[6], (DEPTH, POOL_WIDTH), jnp.float32)
    w_up_pool = jax.random.normal(ks[7], (DEPTH, POOL_WIDTH, D_MODEL), jnp.float32) * POOL_WIDTH ** -0.5
    w_up_attn = jax.random.normal(ks[8], (DEPTH, ATTN_WIDTH, D_MODEL), jnp.float32) * ATTN_WIDTH ** -0.5
    w_out = jax.random.normal(ks[9], (DEPTH, D_MODEL, D_MODEL), jnp.float32) * D_MODEL ** -0.5
    final_norm_g = 1.0 + 0.02 * jax.random.normal(ks[10], (D_MODEL,), jnp.float32)
    return {"x": x, "meta_tokens": meta_tokens, "norm_g": norm_g, "w_in": w_in,
            "b_forget": b_forget, "pool_w": pool_w, "pool_scale": pool_scale,
            "w_up_pool": w_up_pool, "w_up_attn": w_up_attn, "w_out": w_out,
            "final_norm_g": final_norm_g}

def first_block(x, meta_tokens, norm_g, w_in, b_forget, pool_w, pool_scale, w_up_pool, w_up_attn, w_out, final_norm_g):
    B = x.shape[0]
    meta = jnp.broadcast_to(meta_tokens.astype(x.dtype)[None], (B, N_META, D_MODEL))
    h = jnp.concatenate([meta, x], axis=1)
    for l in range(DEPTH):
        h = hybrid_layer(h, norm_g[l], w_in[l], b_forget[l], pool_w[l], pool_scale[l],
                         w_up_pool[l], w_up_attn[l], w_out[l])
    h = rmsnorm(h, final_norm_g)
    return h[:, N_META:]


CHUNK = 64
TOKEN_BLOCK = 128
EPS = 1e-6

SB_HEADS = 8
SB_HEAD_DIM = 64
SB_WIDTH = SB_HEADS * SB_HEAD_DIM

MLA_HEADS = 8
MLA_NOPE_DIM = 64
MLA_ROPE_DIM = 32
MLA_QK_DIM = MLA_NOPE_DIM + MLA_ROPE_DIM
MLA_V_DIM = 64
MLA_Q_RANK = 384
MLA_KV_RANK = 256
MLA_WIDTH = MLA_HEADS * MLA_V_DIM
ROPE_THETA = 10000.0

MIX_WIDTH = SB_WIDTH + MLA_WIDTH
IN_SPLITS = (SB_WIDTH, 2 * SB_WIDTH, 3 * SB_WIDTH,
             3 * SB_WIDTH + MLA_Q_RANK,
             3 * SB_WIDTH + MLA_Q_RANK + MLA_KV_RANK)
IN_PROJ_WIDTH = 3 * SB_WIDTH + MLA_Q_RANK + MLA_KV_RANK + MLA_ROPE_DIM

PEER_HEADS = 8
PEER_N_KEYS = 128
PEER_N_EXPERTS = PEER_N_KEYS * PEER_N_KEYS
PEER_KEY_DIM = 256
PEER_HALF_DIM = PEER_KEY_DIM // 2
PEER_TOPK = 16


def rms_norm(x, g):
    xf = x.astype(jnp.float32)
    y = xf * lax.rsqrt(jnp.mean(xf * xf, axis=-1, keepdims=True) + EPS)
    return (y * g.astype(jnp.float32)).astype(x.dtype)

def rope(x, pos):
    r = x.shape[-1]
    half = r // 2
    inv_freq = 1.0 / (ROPE_THETA ** (jnp.arange(half, dtype=jnp.float32) * (2.0 / r)))
    ang = pos.astype(jnp.float32)[..., None] * inv_freq
    cos = jnp.cos(ang)[:, :, None, :]
    sin = jnp.sin(ang)[:, :, None, :]
    xf = x.astype(jnp.float32)
    x1, x2 = xf[..., :half], xf[..., half:]
    out = jnp.concatenate([x1 * cos - x2 * sin, x1 * sin + x2 * cos], axis=-1)
    return out.astype(x.dtype)

def to_query_blocks(q):
    b, s, h, d = q.shape
    return q.reshape(b, s // Q_BLOCK, Q_BLOCK, h, d).transpose(1, 0, 3, 2, 4)

def from_query_blocks(o):
    nb, b, qb, h, d = o.shape
    return o.transpose(1, 0, 2, 3, 4).reshape(b, nb * qb, h * d)

def stick_breaking_attention(q, k, v):
    b, s, h, d = q.shape
    nb = s // Q_BLOCK
    scale = d ** -0.5
    kpos = jnp.arange(s)

    def block(args):
        qi, bi = args
        z = jnp.einsum('bhqd,bshd->bhqs', qi, k,
                       preferred_element_type=jnp.float32) * scale
        qpos = bi * Q_BLOCK + jnp.arange(Q_BLOCK)
        strict = kpos[None, :] < qpos[:, None]
        log_fail = jnp.where(strict, jax.nn.log_sigmoid(-z), 0.0)
        later = lax.cumsum(log_fail, axis=3, reverse=True) - log_fail
        a = jnp.where(strict, jnp.exp(jax.nn.log_sigmoid(z) + later), 0.0)
        return jnp.einsum('bhqs,bshd->bqhd', a.astype(v.dtype), v)

    out = lax.map(block, (to_query_blocks(q), jnp.arange(nb)))
    return from_query_blocks(out)

def chunk_causal_softmax_attention(q, k, v):
    b, s, h, dq = q.shape
    nb = s // Q_BLOCK
    scale = dq ** -0.5
    kchunk = jnp.arange(s) // CHUNK

    def block(args):
        qi, bi = args
        sc = jnp.einsum('bhqd,bshd->bhqs', qi, k,
                        preferred_element_type=jnp.float32) * scale
        qchunk = (bi * Q_BLOCK + jnp.arange(Q_BLOCK)) // CHUNK
        allowed = kchunk[None, :] <= qchunk[:, None]
        p = jax.nn.softmax(jnp.where(allowed, sc, -jnp.inf), axis=-1)
        return jnp.einsum('bhqs,bshd->bqhd', p.astype(v.dtype), v)

    out = lax.map(block, (to_query_blocks(q), jnp.arange(nb)))
    return from_query_blocks(out)

def peer_ffn(h, w_q, sub_keys, u, v):
    b, s, d = h.shape
    nb = (b * s) // TOKEN_BLOCK
    k = PEER_TOPK

    def block(xt):
        q = (xt @ w_q).reshape(TOKEN_BLOCK, PEER_HEADS, 2, PEER_HALF_DIM)
        sc = jnp.einsum('thcd,chnd->thcn', q, sub_keys,
                        preferred_element_type=jnp.float32)
        top_s, top_i = lax.top_k(sc, k)
        cand_s = top_s[:, :, 0, :, None] + top_s[:, :, 1, None, :]
        cand_i = top_i[:, :, 0, :, None] * PEER_N_KEYS + top_i[:, :, 1, None, :]
        best_s, best_pos = lax.top_k(cand_s.reshape(TOKEN_BLOCK, PEER_HEADS, k * k), k)
        idx = jnp.take_along_axis(cand_i.reshape(TOKEN_BLOCK, PEER_HEADS, k * k),
                                  best_pos, axis=-1)
        g = jax.nn.softmax(best_s, axis=-1)
        pre = jnp.einsum('td,thkd->thk', xt, u[idx], preferred_element_type=jnp.float32)
        coef = (g * jax.nn.gelu(pre, approximate=False)).astype(v.dtype)
        return jnp.einsum('thk,thkd->td', coef, v[idx])

    out = lax.map(block, h.reshape(nb, TOKEN_BLOCK, d))
    return out.reshape(b, s, d)

def second_inputs(seed: int = 0) -> dict:
    key = jax.random.key(seed)
    ks = jax.random.split(key, 20)
    f32 = jnp.float32

    def w(k_, shape, fan_in):
        return jax.random.normal(k_, shape, f32) * (fan_in ** -0.5)

    def gain(k_, shape):
        return 1.0 + 0.02 * jax.random.normal(k_, shape, f32)

    x = jax.random.normal(ks[0], (BATCH, SEQ, D_MODEL), f32)
    offset = jax.random.randint(ks[1], (BATCH, 1), 0, 1024, dtype=jnp.int32)
    positions = (offset + jnp.arange(SEQ, dtype=jnp.int32)[None, :]).astype(jnp.int32)
    return {
        "x": x,
        "positions": positions,
        "attn_norm": gain(ks[2], (DEPTH, D_MODEL)),
        "w_in": w(ks[3], (DEPTH, D_MODEL, IN_PROJ_WIDTH), D_MODEL),
        "cq_norm": gain(ks[4], (DEPTH, MLA_Q_RANK)),
        "w_uq": w(ks[5], (DEPTH, MLA_Q_RANK, MLA_HEADS * MLA_QK_DIM), MLA_Q_RANK),
        "ckv_norm": gain(ks[6], (DEPTH, MLA_KV_RANK)),
        "w_ukv": w(ks[7], (DEPTH, MLA_KV_RANK, MLA_HEADS * (MLA_NOPE_DIM + MLA_V_DIM)), MLA_KV_RANK),
        "q_norm": gain(ks[8], (DEPTH, MLA_QK_DIM)),
        "k_norm": gain(ks[9], (DEPTH, MLA_QK_DIM)),
        "sb_out_norm": gain(ks[10], (DEPTH, SB_WIDTH)),
        "mla_out_norm": gain(ks[11], (DEPTH, MLA_WIDTH)),
        "w_o": w(ks[12], (DEPTH, MIX_WIDTH, D_MODEL), MIX_WIDTH),
        "ffn_norm": gain(ks[13], (DEPTH, D_MODEL)),
        "peer_w_q": w(ks[14], (DEPTH, D_MODEL, PEER_HEADS * PEER_KEY_DIM), D_MODEL),
        "peer_sub_keys": w(ks[15], (DEPTH, 2, PEER_HEADS, PEER_N_KEYS, PEER_HALF_DIM), PEER_HALF_DIM),
        "peer_u": w(ks[16], (DEPTH, PEER_N_EXPERTS, D_MODEL), D_MODEL),
        "peer_v": w(ks[17], (DEPTH, PEER_N_EXPERTS, D_MODEL), D_MODEL),
    }

def second_block(x, positions, attn_norm, w_in, cq_norm, w_uq, ckv_norm, w_ukv, q_norm, k_norm,
              sb_out_norm, mla_out_norm, w_o, ffn_norm, peer_w_q, peer_sub_keys, peer_u, peer_v):
    b, s, _ = x.shape
    for l in range(DEPTH):
        h = rms_norm(x, attn_norm[l])
        proj = h @ w_in[l]
        sb_q, sb_k, sb_v, cq, ckv, k_pe = jnp.split(proj, IN_SPLITS, axis=-1)

        sb = stick_breaking_attention(sb_q.reshape(b, s, SB_HEADS, SB_HEAD_DIM),
                                      sb_k.reshape(b, s, SB_HEADS, SB_HEAD_DIM),
                                      sb_v.reshape(b, s, SB_HEADS, SB_HEAD_DIM))

        q = (rms_norm(cq, cq_norm[l]) @ w_uq[l]).reshape(b, s, MLA_HEADS, MLA_QK_DIM)
        kv = (rms_norm(ckv, ckv_norm[l]) @ w_ukv[l]).reshape(b, s, MLA_HEADS, MLA_NOPE_DIM + MLA_V_DIM)
        k_nope, v = kv[..., :MLA_NOPE_DIM], kv[..., MLA_NOPE_DIM:]
        k_rot = jnp.broadcast_to(k_pe[:, :, None, :], (b, s, MLA_HEADS, MLA_ROPE_DIM))
        k = jnp.concatenate([k_nope, k_rot], axis=-1)
        q = rms_norm(q, q_norm[l])
        k = rms_norm(k, k_norm[l])
        q = jnp.concatenate([q[..., :MLA_NOPE_DIM], rope(q[..., MLA_NOPE_DIM:], positions)], axis=-1)
        k = jnp.concatenate([k[..., :MLA_NOPE_DIM], rope(k[..., MLA_NOPE_DIM:], positions)], axis=-1)
        mla = chunk_causal_softmax_attention(q, k, v)

        mixed = jnp.concatenate([rms_norm(sb, sb_out_norm[l]),
                                 rms_norm(mla, mla_out_norm[l])], axis=-1)
        x = x + mixed @ w_o[l]

        x = x + peer_ffn(rms_norm(x, ffn_norm[l]), peer_w_q[l], peer_sub_keys[l],
                         peer_u[l], peer_v[l])
    return x


def setup_inputs(seed=0):
    out = dict(first_inputs(seed))
    for name, value in second_inputs(seed + 1).items():
        if name != "x":
            out[name + "_2"] = value
    return out


def reference(
    x, meta_tokens, norm_g, w_in, b_forget, pool_w, pool_scale, w_up_pool, w_up_attn, w_out,
    final_norm_g, positions_2, attn_norm_2, w_in_2, cq_norm_2, w_uq_2, ckv_norm_2, w_ukv_2,
    q_norm_2, k_norm_2, sb_out_norm_2, mla_out_norm_2, w_o_2, ffn_norm_2, peer_w_q_2,
    peer_sub_keys_2, peer_u_2, peer_v_2,
):
    x = first_block(
        x, meta_tokens, norm_g, w_in, b_forget, pool_w, pool_scale, w_up_pool, w_up_attn, w_out,
        final_norm_g,
    )
    return second_block(
        x, positions_2, attn_norm_2, w_in_2, cq_norm_2, w_uq_2, ckv_norm_2, w_ukv_2, q_norm_2,
        k_norm_2, sb_out_norm_2, mla_out_norm_2, w_o_2, ffn_norm_2, peer_w_q_2, peer_sub_keys_2,
        peer_u_2, peer_v_2,
    )


_drawn_inputs = setup_inputs


def setup_inputs(seed=0):
    import zlib

    import numpy as np

    out = dict(_drawn_inputs(seed))
    spreads = {}
    factors = {'norm_g': 5.179,
     'attn_norm_2': 2.85,
     'cq_norm_2': 5.763,
     'ckv_norm_2': 3.749,
     'q_norm_2': 5.486,
     'k_norm_2': 6.265,
     'sb_out_norm_2': 5.436,
     'mla_out_norm_2': 5.411,
     'ffn_norm_2': 8.0,
     'peer_w_q_2': 5.318,
     'peer_sub_keys_2': 5.292,
     'peer_u_2': 5.856,
     'peer_v_2': 5.298}
    for name, (base, spread) in spreads.items():
        noise = np.random.default_rng([zlib.crc32(name.encode()), seed]).standard_normal(out[name].shape)
        drawn = base * np.exp(spread * noise) if base else spread * noise
        out[name] = __import__('jax').numpy.asarray(drawn.astype(out[name].dtype))
    for name, factor in factors.items():
        out[name] = (out[name] * factor).astype(out[name].dtype)
    return out
```

```python
from contextlib import ExitStack

import numpy as np

import concourse.bass as bass
from concourse import mybir

ALU = mybir.AluOpType
ACT = mybir.ActivationFunctionType
F32 = mybir.dt.float32
BF16 = mybir.dt.bfloat16
U32 = mybir.dt.uint32
I32 = mybir.dt.int32
AX = mybir.AxisListType.X

P = 128
D = 1024
T = 512
NT = T // P
META = 16
L = META + T
KC = D // P
H = 8
HD = 64
CH = T // P
EPS = 1e-6
NEG = -1e30
BELOW = -3e38

CQ, CKV, ROPE = 384, 256, 32
QK = 96
NK = 128
TOPK = 16
SLOTS = 5
SW = 4096
NB = 10
INV_FREQ = 1.0 / (np.float32(10000.0) ** (np.arange(ROPE // 2, dtype=np.float32) * np.float32(2.0 / ROPE)))
TWO_PI = 2 * np.pi
TP1 = 6.28125
TP2 = float(np.float32(np.round((TWO_PI - TP1) * 2**21) / 2**21))
TP3 = float(np.float32(TWO_PI - TP1 - TP2))
MAGIC = 1.5 * 2**23


def build(nc, a, out):
    ctx = ExitStack()
    with ctx:
        def sb(name, shape, dt=F32):
            return ctx.enter_context(nc.sbuf_tensor("sb_" + name, shape, dt))

        def sem(name):
            return ctx.enter_context(nc.semaphore(name))

        wring = sb("wring", [P, SLOTS, SW])
        ident = sb("ident", [P, P])
        identb = sb("identb", [P, P], BF16)
        masks = sb("masks", [P, 3, P], BF16)
        ones = sb("ones", [P, 1])
        neg_half = sb("neg_half", [P, 2 * H])
        sel8 = sb("sel8", [H, H, P])
        gains = sb("gains", [P, 64])
        gain_row = sb("gain_row", [P, D])
        qk_gain = sb("qk_gain", [P, 2, QK])
        stat = sb("stat", [P, 128])
        negc = sb("negc", [H, L])
        freq = sb("freq", [P, ROPE // 2])
        trig = sb("trig", [P, 2, NT, ROPE // 2])
        posi = sb("posi", [P, NT], I32)
        posf = sb("posf", [P, NT])
        idx = sb("idx", [P, 2, H * TOPK], U32)
        iota = sb("iota", [P, TOPK])
        angle = sb("angle", [P, 2, NT * ROPE // 2])
        AW = nc.sbuf_bytes_remaining // 4 - 16
        arena = sb("arena", [P, AW])
        psum = ctx.enter_context(nc.psum_tensor("ps", [P, 8, 512], F32))

        def cut(at, *shape):
            n = int(np.prod(shape))
            assert at + n <= AW, (at, n, AW)
            v = arena[:, at:at + n]
            if len(shape) == 2:
                v = v.rearrange("p (a b) -> p a b", a=shape[0])
            elif len(shape) == 3:
                v = v.rearrange("p (a b c) -> p a b c", a=shape[0], b=shape[1])
            return v

        at = 0
        hT = cut(at, KC, L); at += KC * L
        qT = cut(at, CH, T); at += CH * T
        kT = cut(at, CH, L); at += CH * L
        vtok = cut(at, NT, T); at += NT * T
        vmeta = cut(at, T); at += T
        za = cut(at, CH, T); at += CH * T
        zp = cut(at, CH, T); at += CH * T
        gates_at = at
        gate = cut(at, 2, KC, T); at += 2 * KC * T
        Pb = cut(at, 2, L); at += 2 * L
        PT = cut(at, 2, 5, P); at += 2 * 5 * P
        xs = cut(gates_at, NT, D)
        xmeta = cut(gates_at + NT * D, D)
        uT = cut(gates_at, CH, L)
        win = cut(gates_at + CH * L, 2, L)
        lf = cut(gates_at + CH * L + 2 * L, 3, L)
        poolw = cut(gates_at + 6 * D, CH, P)
        f_w = cut(gates_at + 6 * D + CH * P, KC, H)
        junk = cut(gates_at + 7 * D, D)
        at2 = 0
        x1 = cut(at2, NT, D); at2 += NT * D
        hx = at2
        x2T = cut(at2, KC, T); at2 += KC * T
        sq = cut(at2, CH, T); at2 += CH * T
        sk = cut(at2, CH, T); at2 += CH * T
        sv = cut(at2, NT, T); at2 += NT * T
        mq = cut(at2, H, T); at2 += H * T
        mk = cut(at2, H, T); at2 += H * T
        mv = cut(at2, NT, T); at2 += NT * T
        scratch = at2
        xn2 = cut(scratch, 2, D)
        cqt = cut(scratch, NT, CQ + CKV + ROPE)
        latT = cut(scratch + NT * 672, 10, P)
        rows = cut(hx, 2, H, QK)
        rsq = cut(hx + 2 * H * QK, 2, H, QK)
        rtmp = cut(hx + 2 * H * QK, 4, H * (ROPE // 2))
        og = cut(hx, 2 * CH, T)
        Pb2 = cut(scratch, 2, T)
        PT2 = cut(scratch + 2 * T, 2, 4, P)
        st = cut(scratch + 4 * T, 3, T)
        osq = cut(scratch + 7 * T, 2, P)
        at3 = NT * D
        xn = cut(at3, 2, D); at3 += 2 * D
        xnT = cut(at3, KC, P); at3 += KC * P
        pq = cut(at3, 2 * H, P); at3 += 2 * H * P
        skT = cut(at3, 2 * H, P); at3 += 2 * H * P
        sc = cut(at3, 2 * H, P); at3 += 2 * H * P
        sc2 = cut(at3, 256); at3 += 256
        cand = cut(at3, 256); at3 += 256
        cand2 = cut(at3, 256); at3 += 256
        tops = cut(at3, 2 * H, TOPK); at3 += 2 * H * TOPK
        best = cut(at3, H, TOPK); at3 += H * TOPK
        topif = cut(at3, 2 * H, TOPK); at3 += 2 * H * TOPK
        posf2 = cut(at3, 2, H * TOPK); at3 += 2 * H * TOPK
        idxf = cut(at3, 3, H * TOPK); at3 += 3 * H * TOPK
        onehot = sc.rearrange("p a (b c) -> p (a b) c", c=TOPK)
        topi = cut(at3, 2 * H, TOPK).bitcast(U32); at3 += 2 * H * TOPK
        posn = cut(at3, H, TOPK).bitcast(U32); at3 += H * TOPK
        posab = cut(at3, 2, H * TOPK).bitcast(U32); at3 += 2 * H * TOPK
        soft = cut(at3, 2, H * TOPK); at3 += 2 * H * TOPK
        pre = cut(at3, H * TOPK); at3 += H * TOPK
        gel = cut(at3, H * TOPK); at3 += H * TOPK
        coef = cut(at3, H * TOPK); at3 += H * TOPK
        diag = cut(at3, 4, P); at3 += 4 * P
        ostage = cut(at3, D); at3 += D
        gbuf = cut(at3, NB, D); at3 += NB * D

        rsq_junk = cut(gates_at + 7 * D, D)
        GN, GP, GA2, GC, GKV, GSB, GML = 0, 8, 12, 20, 23, 25, 29

        w_landed = [sem(f"w_landed{i}") for i in range(SLOTS)]
        x_in = sem("x_in"); small_in = sem("small_in"); xres_in = sem("xres_in"); grow_in = sem("grow_in")
        consts = sem("consts"); pool_chain = sem("pool_chain")
        dense_done = sem("dense_done"); act_evac = sem("act_evac"); dve_evac = sem("dve_evac")
        act_chain = sem("act_chain"); dve_chain = sem("dve_chain")
        ss_done = sem("ss_done"); rstd_done = sem("rstd_done"); ms_done = sem("ms_done")
        xn_done = sem("xn_done")
        tanh_done = sem("tanh_done"); pooled = sem("pooled"); decay_x = sem("decay_x")
        decay_ln = sem("decay_ln"); decay_done = sem("decay_done")
        s_done = sem("s_done"); max_done = sem("max_done"); exp_done = sem("exp_done")
        norm_done = sem("norm_done"); pT_done = sem("pT_done"); pT_copied = sem("pT_copied")
        pv_done = sem("pv_done"); y_done = sem("y_done")
        merged_done = sem("merged_done"); x1_done = sem("x1_done")
        rope_arg = sem("rope_arg"); trig_done = sem("trig_done")
        row_sq = sem("row_sq"); rows_squared = sem("rows_squared"); rope_done = sem("rope_done")
        osq_done = sem("osq_done"); og_done = sem("og_done"); oss_done = sem("oss_done")
        oms_done = sem("oms_done"); orstd_done = sem("orstd_done")
        z_abs = sem("z_abs"); sp_done = sem("sp_done"); zr_done = sem("zr_done")
        wo_done = sem("wo_done"); x2_done = sem("x2_done")
        p_ss = sem("p_ss"); p_rstd = sem("p_rstd"); p_xn = sem("p_xn"); prep_mm = sem("prep_mm")
        prep_evac = sem("prep_evac"); soft_in = sem("soft_in"); soft_exp = sem("soft_exp")
        idx_ready = sem("idx_ready"); tile_state = sem("tile_state")
        landed = [sem(f"gathered{i}") for i in range(NB)]
        u_used = sem("u_used"); v_used = sem("v_used"); gelu_done = sem("gelu_done")
        coef_done = sem("coef_done"); diag_done = sem("diag_done"); acc_done = sem("acc_done")
        acc_read = sem("acc_read"); x2_half = sem("x2_half"); out_sent = sem("out_sent")

        plan, index = [], {}

        def group(tag, bank, by):
            index[tag] = len(plan)
            plan.append((bank, by))

        turn = [0]

        def ring(tag, by, banks=8):
            group(tag, turn[0] % banks, by)
            turn[0] += 1

        evac_sem = {"A": act_evac, "V": dve_evac}

        def evac_count(tag):
            n = index[tag]
            by = plan[n][1]
            return evac_sem[by], sum(b == by for _, b in plan[:n + 1])

        def wait_evac(eng, tag):
            s, n = evac_count(tag)
            eng.wait_ge(s, n)

        def wait_group(eng, tag):
            eng.wait_ge(dense_done, index[tag] + 1)

        def bank(tag):
            return psum[:, plan[index[tag]][0], :]

        def wait_bank(pe, tag):
            n = index[tag]
            before = [m for m in range(n) if plan[m][0] == plan[n][0]]
            if before:
                by = plan[before[-1]][1]
                pe.wait_ge(evac_sem[by], sum(b == by for _, b in plan[:before[-1] + 1]))

        for c in range(KC):
            ring(f"hT{c}", "AV"[c % 2])
        ring("hTm", "V")
        for c in range(CH):
            ring(f"zp{c}", "V")
        for c in range(CH):
            ring(f"u{c}", "A")
        ring("um", "V")
        for c in range(CH):
            ring(f"k{c}", "A")
        ring("km", "V")
        ring("f", "V")
        ring("fm", "V")
        for c in range(CH):
            ring(f"q{c}", "A")
        for t in range(NT):
            ring(f"v{t}", "A")
        ring("vm", "V")
        for c in range(CH):
            ring(f"pm{c}", "V")
        for c in range(CH):
            ring(f"za{c}", "V")
        before_attention = len(plan)
        GATES = [(s, c) for s in range(2) for c in range(KC)]
        for s, c in GATES:
            group(f"g{s}{c}", 7, "A")
        for c in range(KC):
            ring(f"up0{c}", "V")
            ring(f"up1{c}", "V")
        for t in range(NT):
            for e in range(2):
                ring(f"y{t}{e}", "V")
            for j in range(2):
                if t:
                    ring(f"x2T{t - 1}{j}", "V")
        for j in range(2):
            ring(f"x2T{NT - 1}{j}", "V")
        for c in range(CH):
            ring(f"sq{c}", "A")
        for c in range(CH):
            ring(f"sk{c}", "A")
        for t in range(NT):
            ring(f"sv{t}", "A")
        for t in range(NT):
            ring(f"cq{t}", "A")
            ring(f"ckv{t}", "A")
        ring("cqT0", "V")
        ring("ckvT0", "V")
        for t in range(NT):
            for j in range(2):
                ring(f"uq{t}{j}", "A")
            for j in range(2):
                ring(f"ukv{t}{j}", "A")
            if t + 1 < NT:
                ring(f"cqT{t + 1}", "V")
                ring(f"ckvT{t + 1}", "V")
            for j in range(2):
                for g in range(2):
                    ring(f"qkT{t}{j}{g}", "A")
        all_dense_a = sum(b == "A" for _, b in plan)
        all_dense_v = sum(b == "V" for _, b in plan)

        w_in = a["w_in"][0]
        w_in2 = a["w_in_2"][0]

        def chunks(w):
            return w.rearrange("(c p) n -> p c n", p=P)

        U, Z, Q, K, V, ZA, F, G0, G1 = 0, 512, 1024, 1536, 2048, 2560, 3072, 3080, 4104
        units = [("zp", chunks(w_in[:, Z:Z + 512])), ("u", chunks(w_in[:, U:U + 512])),
                 ("k", chunks(w_in[:, K:K + 512])), ("q", chunks(w_in[:, Q:Q + 512])),
                 ("v", chunks(w_in[:, V:V + 512])), ("za", chunks(w_in[:, ZA:ZA + 512]))]
        last_use = {"zp": "zp3", "u": "um", "k": "km", "q": "q3", "v": "vm", "za": "za3"}
        for s, g0 in enumerate((G0, G1)):
            for j in range(2):
                units.append((f"g{s}{j}", chunks(w_in[:, g0 + 512 * j:g0 + 512 * j + 512])))
                last_use[f"g{s}{j}"] = f"g{s}{4 * j + 3}"
        units += [("wup0", chunks(a["w_up_pool"][0])), ("wup1", chunks(a["w_up_attn"][0]))]
        last_use["wup0"] = last_use["wup1"] = "up17"
        for j in range(2):
            units.append((f"wout{j}", chunks(a["w_out"][0][512 * j:512 * j + 512])))
            last_use[f"wout{j}"] = "y31"
        units += [("sq", chunks(w_in2[:, 0:512])), ("sk", chunks(w_in2[:, 512:1024])),
                  ("sv", chunks(w_in2[:, 1024:1536])), ("cq", chunks(w_in2[:, 1536:1920])),
                  ("ckv", chunks(w_in2[:, 1920:2208])), ("uq", chunks(a["w_uq_2"][0])),
                  ("ukv", chunks(a["w_ukv_2"][0]))]
        last_use |= {"sq": "sq3", "sk": "sk3", "sv": "sv3", "cq": "cq3", "ckv": "ckv3",
                     "uq": "uq31", "ukv": "ukv31"}
        for j in range(2):
            units.append((f"wo{j}", chunks(a["w_o_2"][0][512 * j:512 * j + 512])))
        units.append(("subk", a["peer_sub_keys_2"][0].rearrange("c h n d -> n (c h) d")))
        for j in range(4):
            units.append((f"pq{j}", chunks(a["peer_w_q_2"][0][:, 512 * j:512 * j + 512])))
        unit = {name: n for n, (name, _) in enumerate(units)}

        def weights(name):
            n = unit[name]
            _, src = units[n]
            c, w = src.shape[1], src.shape[2]
            return wring[:, n % SLOTS, 0:c * w].rearrange("p (c w) -> p c w", c=c)

        def wait_weights(pe, name):
            n = unit[name]
            pe.wait_ge(w_landed[n % SLOTS], 16 * (n // SLOTS + 1))

        ATT1 = [(i, h) for i in range(NT) for h in range(H)]
        ATT2 = [(i, kind, h) for i in range(NT) for kind in range(2) for h in range(H)]
        N1, N2 = len(ATT1), len(ATT2)

        def ml_count(m):
            return H * (m // 16) + m % 16 - H + 1

        def meta_ps(n, i):
            if i < NT - 1:
                return psum[0:META, 4 + n % 2, 3 * P:4 * P]
            return psum[0:META, 2 * (n % 2) + 1, P:2 * P]

        CHUNKS = NT * H
        GATHERS = 2 * CHUNKS * TOPK

        def gather_of(g):
            if g < TOPK:
                return "u", 0, g
            k, j = divmod(g - TOPK, 2 * TOPK)
            if k < CHUNKS - 1 and j < TOPK:
                k, kind = k + 1, "u"
            else:
                kind = "v"
            return kind, k // H, (k % H) * TOPK + j % TOPK

        def u_gather(t, s):
            k = H * t + s // TOPK
            return (TOPK + 2 * TOPK * (k - 1) if k else 0) + s % TOPK

        def v_gather(t, s):
            k = H * t + s // TOPK
            return TOPK + 2 * TOPK * k + (TOPK if k < CHUNKS - 1 else 0) + s % TOPK

        PREP = [("xT", 0), ("xT", 1)] + [("q", j) for j in range(4)] + [("s", 0), ("s", 2), ("s", 1), ("s", 3)]
        SUBK_GROUPS = 4
        PREP_AT = [(0, 1), (2, 3), (4, 5), (6, 7, 8, 9), (), (), (), ()]
        TOP_AT = [(), (), (), (), (0, 1, 2), (3, 4, 5), (6, 7), ()]
        SOFT_AT = 6
        SMALL = 16 * 14

        block = ctx.enter_context(nc.Block())

        @block.sync
        def _(sp):
            for n, (name, src) in enumerate(units):
                if n >= SLOTS:
                    old = units[n - SLOTS][0]
                    if old in last_use:
                        sp.wait_ge(dense_done, index[last_use[old]] + 1)
                    else:
                        sp.wait_ge(wo_done, 2 * NT)
                sp.dma_start(weights(name), src).then_inc(w_landed[n % SLOTS], 16)
            for t in range(NT):
                sp.wait_ge(acc_read, t + 1)
                sp.dma_start(out[0, t * P:(t + 1) * P, :], ostage[:]).then_inc(out_sent, 16)
            sp.wait_ge(out_sent, 16 * NT)

        @block.gpsimd
        def _(gp):
            count = [0]

            def link(ins):
                count[0] += 1
                ins.then_inc(pool_chain, 1)
                gp.wait_ge(pool_chain, count[0])

            nc.gpsimd.memset(ones[:], 1.0)
            nc.gpsimd.memset(neg_half[:], -0.5)
            nc.gpsimd.memset(sel8[:], 0.0)
            nc.gpsimd.memset(masks[:], 0.0)
            for j in range(ROPE // 2):
                nc.gpsimd.memset(freq[:, j:j + 1], float(INV_FREQ[j]))
            nc.gpsimd.memset(identb[:], 0.0)
            link(nc.gpsimd.memset(ident[:], 0.0))
            for m in (ident, identb):
                nc.gpsimd.affine_select(out=m[:], in_=m[:], compare_op=ALU.not_equal, fill=1.0, base=0,
                                        pattern=[[-1, P]], channel_multiplier=1)
            nc.gpsimd.affine_select(out=sel8[:], in_=sel8[:], compare_op=ALU.not_equal, fill=1.0, base=0,
                                    pattern=[[-1, H], [0, P]], channel_multiplier=1)
            for m in range(2):
                nc.gpsimd.affine_select(out=masks[:, m, :], in_=masks[:, m, :], compare_op=ALU.is_ge, fill=NEG,
                                        base=-m, pattern=[[-1, P]], channel_multiplier=1)
            nc.gpsimd.iota(iota[:], [[1, TOPK]], base=0, channel_multiplier=0,
                           allow_small_or_imprecise_dtypes=True)
            link(nc.gpsimd.memset(masks[0:64, 2, 64:P], NEG))
            gp.sem_inc(consts, 1)

            def rstd(ss_ap, out_ap, wait_s, wait_n, scale=1.0):
                gp.wait_ge(wait_s, wait_n)
                link(nc.gpsimd.tensor_scalar(ss_ap, ss_ap, scale, EPS, ALU.mult, ALU.add))
                rows, n = ss_ap.shape
                return nc.gpsimd.tensor_tensor(out_ap, ss_ap, neg_half[0:rows, 0:n], ALU.pow)

            rstd(stat[:, 0:4], stat[:, 8:12], ss_done, 5).then_inc(rstd_done, 1)
            rstd(stat[0:META, 4:5], stat[0:META, 12:13], ss_done, 5).then_inc(rstd_done, 1)
            for t in range(NT):
                rstd(stat[:, 16 + t:17 + t], stat[:, 20 + t:21 + t], ms_done, 2 * t + 1).then_inc(rstd_done, 1)
                rstd(stat[:, 24 + t:25 + t], stat[:, 28 + t:29 + t], ms_done, 2 * t + 2).then_inc(rstd_done, 1)
            for t in range(NT):
                rstd(stat[:, 32 + t:33 + t], stat[:, 40 + t:41 + t], ms_done, 2 * NT + 2 * t + 2, 1.0 / CQ)\
                    .then_inc(rstd_done, 1)
                rstd(stat[:, 36 + t:37 + t], stat[:, 44 + t:45 + t], ms_done, 2 * NT + 2 * t + 2, 1.0 / CKV)\
                    .then_inc(rstd_done, 1)
            for t in range(NT):
                rstd(stat[:, 48:64], stat[:, 64:80], row_sq, 2 * t + 2, 1.0 / QK).then_inc(rstd_done, 1)
            for t in range(NT):
                rstd(stat[:, 80:82], stat[:, 82:84], oms_done, t + 1, 1.0 / T).then_inc(orstd_done, 1)

            rstd(stat[:, 84:88], stat[:, 88:92], p_ss, NT).then_inc(p_rstd, 1)
            for g in range(GATHERS):
                kind, t, s = gather_of(g)
                if kind == "u" and s == 0:
                    gp.wait_ge(idx_ready, t + 1)
                if g >= NB:
                    was, wt, ws = gather_of(g - NB)
                    gp.wait_ge(u_used if was == "u" else v_used, H * TOPK * wt + ws + 1)
                table = a["peer_u_2" if kind == "u" else "peer_v_2"][0]
                nc.gpsimd.indirect_dma_start(gbuf[:, g % NB, :], None, table,
                                             bass.IndirectOffsetOnAxis(ap=idx[:, t % 2, s:s + 1], axis=0))\
                    .then_inc(landed[g % NB], 16)

        @block.scalar
        def _(act):
            done = [0]
            count = [0]

            def link(ins):
                count[0] += 1
                ins.then_inc(act_chain, 1)
                act.wait_ge(act_chain, count[0])

            def freed(ins, tag):
                done[0] += 1
                assert evac_count(tag) == (act_evac, done[0]), tag
                ins.then_inc(act_evac, 1)

            for t in range(NT):
                act.dma_start(xs[:, t, :], a["x"][0, t * P:(t + 1) * P, :]).then_inc(x_in, 16)
            act.dma_start(xmeta[0:META, :], a["meta_tokens"]).then_inc(x_in, 16)

            def column(at, n, src):
                act.dma_start(gains[:, at:at + n], src.rearrange("(c p) -> p c", p=P),
                              allow_slow_non_contiguous=True).then_inc(small_in, 16)

            column(GN, 8, a["norm_g"][0])
            column(GP, 4, a["pool_scale"][0])
            column(GA2, 8, a["attn_norm_2"][0])
            column(GC, 3, a["cq_norm_2"][0])
            column(GKV, 2, a["ckv_norm_2"][0])
            column(GSB, 4, a["sb_out_norm_2"][0])
            column(GML, 4, a["mla_out_norm_2"][0])
            act.dma_start(gains[0:H, 40:41], a["b_forget"].rearrange("a h -> h a"),
                          allow_slow_non_contiguous=True).then_inc(small_in, 16)
            act.dma_start(f_w[:], chunks(w_in[:, F:F + H]), allow_slow_non_contiguous=True).then_inc(small_in, 16)
            act.dma_start(poolw[:], a["pool_w"][0].rearrange("g c d -> c g d")).then_inc(small_in, 16)
            act.dma_start(posi[:], a["positions_2"].rearrange("a (t p) -> p (a t)", p=P),
                          allow_slow_non_contiguous=True).then_inc(small_in, 16)
            act.dma_start(gain_row[:], a["final_norm_g"].partition_broadcast(P)).then_inc(small_in, 16)
            act.dma_start(qk_gain[:, 0, :], a["q_norm_2"][0].partition_broadcast(P)).then_inc(small_in, 16)
            act.dma_start(qk_gain[:, 1, :], a["k_norm_2"][0].partition_broadcast(P)).then_inc(small_in, 16)

            act.wait_ge(x_in, 16 * (NT + 1))
            for t in range(NT):
                if t:
                    act.wait_ge(ss_done, t)
                nc.scalar.activation(junk[:], xs[:, t, :], ACT.Square, scale=1 / 32,
                                     accum_out=stat[:, t:t + 1]).then_inc(ss_done, 1)
            act.wait_ge(ss_done, NT)
            nc.scalar.activation(junk[0:META, :], xmeta[0:META, :], ACT.Square, scale=1 / 32,
                                 accum_out=stat[0:META, 4:5]).then_inc(ss_done, 1)
            act.wait_ge(small_in, SMALL)
            for c in range(0, KC, 2):
                wait_group(act, f"hT{c}")
                freed(nc.scalar.activation(hT[:, c, META:L], bank(f"hT{c}"), ACT.Copy,
                                           scale=gains[:, GN + c:GN + c + 1]), f"hT{c}")
            for c in range(CH):
                wait_group(act, f"zp{c}")
                nc.scalar.activation(zp[:, c, :], bank(f"zp{c}"), ACT.Tanh, scale=0.5).then_inc(tanh_done, 1)
            act.wait_ge(xn_done, NT + 1)
            wait_group(act, "hTm")
            for c in range(CH):
                wait_group(act, f"u{c}")
                freed(nc.scalar.copy(uT[:, c, META:L], bank(f"u{c}")), f"u{c}")
            for c in range(CH):
                wait_group(act, f"k{c}")
                freed(nc.scalar.copy(kT[:, c, META:L], bank(f"k{c}")), f"k{c}")
            act.wait_ge(decay_x, 1)
            link(nc.scalar.activation(lf[0:H, 1, :], lf[0:H, 0, :], ACT.Abs))
            link(nc.scalar.activation(lf[0:H, 1, :], lf[0:H, 1, :], ACT.Exp, scale=-1.0))
            nc.scalar.activation(lf[0:H, 1, :], lf[0:H, 1, :], ACT.Ln, bias=1.0).then_inc(decay_ln, 1)
            for c in range(CH):
                wait_group(act, f"q{c}")
                freed(nc.scalar.activation(qT[:, c, :], bank(f"q{c}"), ACT.Copy, scale=HD ** -0.5), f"q{c}")
            for t in range(NT):
                wait_group(act, f"v{t}")
                freed(nc.scalar.copy(vtok[:, t, :], bank(f"v{t}")), f"v{t}")
            for c in range(CH):
                wait_group(act, f"za{c}")
                nc.scalar.activation(za[:, c, :], bank(f"za{c}"), ACT.Tanh, scale=0.5).then_inc(tanh_done, 1)

            def copy_pT(n, i):
                act.wait_ge(pT_done, n + 1)
                if n >= 2:
                    act.wait_ge(pv_done, n - 1)
                w = (i + 1) * P
                nc.scalar.copy(PT[:, n % 2, 0:i + 1, :],
                               psum[:, 4 + n % 2, 0:w].rearrange("p (a b) -> p a b", b=P))
                nc.scalar.copy(PT[0:META, n % 2, 4, :], meta_ps(n, i)).then_inc(pT_copied, 1)

            act.wait_ge(pooled, 1 + CH)
            for n, (i, h) in enumerate(ATT1):
                w = (i + 1) * P + META
                act.wait_ge(max_done, n + 1)
                if n >= 2:
                    act.wait_ge(pT_done, n - 1)
                s_ps = psum[:, 2 * (n % 2):2 * (n % 2) + 2, :].rearrange("p a b -> p (a b)")
                nc.scalar.activation(Pb[:, n % 2, 0:w], s_ps[:, 0:w], ACT.Exp, bias=stat[:, 96 + n % 4:97 + n % 4],
                                     accum_out=stat[:, 100 + n % 4:101 + n % 4]).then_inc(exp_done, 1)
                if n:
                    copy_pT(n - 1, ATT1[n - 1][0])
                if n % 2 == 1:
                    s, c = GATES[n // 2]
                    wait_group(act, f"g{s}{c}")
                    freed(nc.scalar.activation(gate[:, s, c, :], bank(f"g{s}{c}"), ACT.Tanh, scale=0.5), f"g{s}{c}")
            copy_pT(N1 - 1, NT - 1)
            for t in range(NT):
                act.dma_start(x1[:, t, :], a["x"][0, t * P:(t + 1) * P, :]).then_inc(xres_in, 16)

            nc.scalar.preload_act_table_set("natural_log_exp_and_others")
            for t in range(NT):
                act.wait_ge(x1_done, 2 * t + 1)
                nc.scalar.activation(junk[:], x1[:, t, :], ACT.Square, scale=1 / 32,
                                     accum_out=stat[:, 16 + t:17 + t]).then_inc(ms_done, 1)
                act.wait_ge(x1_done, 2 * t + 2)
                act.wait_ge(ms_done, 2 * t + 1)
                nc.scalar.activation(junk[:], x1[:, t, :], ACT.Square, scale=1 / 32,
                                     accum_out=stat[:, 24 + t:25 + t]).then_inc(ms_done, 1)
                act.wait_ge(ms_done, 2 * t + 2)
            act.dma_start(gain_row[:], a["ffn_norm_2"][0].partition_broadcast(P)).then_inc(grow_in, 16)

            act.wait_ge(rope_arg, 1)
            nc.scalar.activation(trig[:], trig[:], ACT.Sin).then_inc(trig_done, 1)
            nc.scalar.preload_act_table_set("natural_log_exp_and_others")
            for c in range(CH):
                wait_group(act, f"sq{c}")
                freed(nc.scalar.activation(sq[:, c, :], bank(f"sq{c}"), ACT.Copy, scale=HD ** -0.5), f"sq{c}")
            for c in range(CH):
                wait_group(act, f"sk{c}")
                freed(nc.scalar.copy(sk[:, c, :], bank(f"sk{c}")), f"sk{c}")
            for t in range(NT):
                wait_group(act, f"sv{t}")
                freed(nc.scalar.copy(sv[:, t, :], bank(f"sv{t}")), f"sv{t}")
            wait_group(act, "x2T31")
            for t in range(NT):
                wait_group(act, f"cq{t}")
                nc.scalar.copy(cqt[:, t, 0:CQ], bank(f"cq{t}")[:, 0:CQ])
                nc.scalar.activation(rsq_junk[:, 0:CQ], bank(f"cq{t}")[:, 0:CQ], ACT.Square,
                                     accum_out=stat[:, 32 + t:33 + t]).then_inc(ms_done, 1)
                act.wait_ge(ms_done, 2 * NT + 2 * t + 1)
                act.sem_inc(act_evac, 1)
                wait_group(act, f"ckv{t}")
                nc.scalar.copy(cqt[:, t, CQ:672], bank(f"ckv{t}")[:, 0:CKV + ROPE])
                nc.scalar.activation(rsq_junk[:, 0:CKV], bank(f"ckv{t}")[:, 0:CKV], ACT.Square,
                                     accum_out=stat[:, 36 + t:37 + t]).then_inc(ms_done, 1)
                act.wait_ge(ms_done, 2 * NT + 2 * t + 2)
                act.sem_inc(act_evac, 1)
                done[0] += 2
            wait_group(act, "ckv3")
            for t in range(NT):
                for j in range(2):
                    wait_group(act, f"uq{t}{j}")
                    if t and not j:
                        wait_group(act, f"qkT{t - 1}11")
                        act.wait_ge(rope_done, 2 * t)
                    freed(nc.scalar.copy(rows[:, 0, 4 * j:4 * j + 4, :],
                                         bank(f"uq{t}{j}")[:, 0:4 * QK].rearrange("p (h d) -> p h d", h=4)),
                          f"uq{t}{j}")
                for j in range(2):
                    wait_group(act, f"ukv{t}{j}")
                    kv = bank(f"ukv{t}{j}").rearrange("p (h d) -> p h d", h=4)
                    nc.scalar.copy(rows[:, 1, 4 * j:4 * j + 4, 0:HD], kv[:, :, 0:HD])
                    freed(nc.scalar.copy(mv[:, t, :].rearrange("p (h d) -> p h d", h=H)[:, 4 * j:4 * j + 4, :],
                                         kv[:, :, HD:P]), f"ukv{t}{j}")
                link(nc.scalar.copy(rows[:, 1, :, HD:QK],
                                    cqt[:, t, CQ + CKV:672].unsqueeze(1).to_broadcast([P, H, ROPE])))
                for j in range(2):
                    nc.scalar.activation(rsq[:, j], rows[:, j], ACT.Square).then_inc(rows_squared, 1)
                for j in range(2):
                    for g in range(2):
                        wait_group(act, f"qkT{t}{j}{g}")
                        dst = (mq, mk)[j]
                        freed(nc.scalar.copy(dst[0:QK, 4 * g:4 * g + 4, t * P:(t + 1) * P],
                                             bank(f"qkT{t}{j}{g}")[0:QK, :].rearrange("p (h t) -> p h t", h=4)),
                              f"qkT{t}{j}{g}")

            def copy_pT2(m):
                i = ATT2[m][0]
                act.wait_ge(pT_done, N1 + m + 1)
                if m >= 2:
                    act.wait_ge(pv_done, N1 + m - 1)
                nc.scalar.copy(PT2[:, m % 2, 0:i + 1, :],
                               psum[:, 4 + m % 2, 0:(i + 1) * P].rearrange("p (a b) -> p a b", b=P))\
                    .then_inc(pT_copied, 1)

            def squares(m):
                i, kind, h = ATT2[m]
                act.wait_ge(pv_done, N1 + m + 1)
                if pair_of(m) >= 2:
                    act.wait_ge(oss_done, pair_of(m) - 1)
                nc.scalar.activation(osq[:, pair_of(m) % 2, :], psum[:, 6, 0:P], ACT.Square).then_inc(osq_done, 1)

            def pair_of(m):
                return m // 2

            sb_n = 0
            for m, (i, kind, h) in enumerate(ATT2):
                w = (i + 1) * P
                s_ps = psum[:, 2 * (m % 2), 0:w]
                if kind == 0:
                    act.wait_ge(s_done, N1 + m + 1)
                    if sb_n:
                        act.wait_ge(zr_done, sb_n)
                    nc.scalar.activation(st[:, 0, 0:w], s_ps, ACT.Abs).then_inc(z_abs, 1)
                    act.wait_ge(z_abs, sb_n + 1)
                    link(nc.scalar.activation(st[:, 0, 0:w], st[:, 0, 0:w], ACT.Exp, scale=-1.0))
                    nc.scalar.activation(st[:, 0, 0:w], st[:, 0, 0:w], ACT.Ln, bias=1.0).then_inc(sp_done, 1)
                    sb_n += 1
                    if m:
                        copy_pT2(m - 1)
                    act.wait_ge(zr_done, sb_n)
                    if m >= 2:
                        act.wait_ge(pT_done, N1 + m - 1)
                    nc.scalar.activation(Pb2[:, m % 2, 0:w], st[:, 1, 0:w], ACT.Exp).then_inc(exp_done, 1)
                else:
                    act.wait_ge(max_done, N1 + ml_count(m))
                    if m >= 2:
                        act.wait_ge(pT_done, N1 + m - 1)
                    nc.scalar.activation(Pb2[:, m % 2, 0:w], s_ps, ACT.Exp, bias=stat[:, 96 + m % 4:97 + m % 4],
                                         scale=QK ** -0.5, accum_out=stat[:, 100 + m % 4:101 + m % 4])\
                        .then_inc(exp_done, 1)
                    if m:
                        copy_pT2(m - 1)
                if m >= 2 and m % 2 == 1:
                    squares(m - 2)
            copy_pT2(N2 - 1)
            squares(N2 - 1)

            act.wait_ge(x2_done, NT)
            for t in range(NT):
                if t:
                    act.wait_ge(p_ss, t)
                nc.scalar.activation(ostage[:], x1[:, t, :], ACT.Square, scale=1 / 32,
                                     accum_out=stat[:, 84 + t:85 + t]).then_inc(p_ss, 1)

            def evac_prep(t, n):
                kind, j = PREP[n]
                act.wait_ge(prep_mm, SUBK_GROUPS + len(PREP) * t + n + 1)
                src = psum[:, 4 + (SUBK_GROUPS + len(PREP) * t + n) % 4, :].rearrange("p (a b) -> p a b", b=P)
                dst = {"xT": xnT, "q": pq, "s": sc}[kind][:, 4 * j:4 * j + 4, :]
                nc.scalar.copy(dst, src).then_inc(prep_evac, 1)

            for j in range(SUBK_GROUPS):
                act.wait_ge(prep_mm, j + 1)
                nc.scalar.copy(skT[:, 4 * j:4 * j + 4, :],
                               psum[:, 4 + j % 4, :].rearrange("p (a b) -> p a b", b=P)).then_inc(prep_evac, 1)
            for n in range(len(PREP)):
                evac_prep(0, n)

            def exp_soft(t):
                act.wait_ge(soft_in, t + 1)
                nc.scalar.activation(soft[:, t % 2, :], soft[:, t % 2, :], ACT.Exp).then_inc(soft_exp, 1)

            exp_soft(0)

            def gelu_part(t, c):
                act.wait_ge(u_used, (H * t + c + 1) * TOPK)
                nc.scalar.activation(gel[:, c * TOPK:(c + 1) * TOPK], pre[:, c * TOPK:(c + 1) * TOPK], ACT.Gelu)\
                    .then_inc(gelu_done, 1)

            def diagonals(t, c):
                act.wait_ge(coef_done, H * t + c + 1)
                for s in range(c * TOPK, (c + 1) * TOPK):
                    n = H * TOPK * t + s
                    if n >= 4:
                        act.wait_ge(v_used, n - 3)
                    nc.scalar.activation(diag[:, n % 4, :], ident[:], ACT.Copy, scale=coef[:, s:s + 1])\
                        .then_inc(diag_done, 1)

            for t in range(NT):
                for c in range(H):
                    gelu_part(t, c)
                    if t + 1 < NT and c == SOFT_AT:
                        exp_soft(t + 1)
                    diagonals(t, c)
                    if t + 1 < NT:
                        for n in PREP_AT[c]:
                            evac_prep(t + 1, n)

        @block.vector
        def _(dve):
            done = [0]
            count = [0]

            def link(ins):
                count[0] += 1
                ins.then_inc(dve_chain, 1)
                dve.wait_ge(dve_chain, count[0])

            def freed(ins, tag):
                done[0] += 1
                assert evac_count(tag) == (dve_evac, done[0]), tag
                ins.then_inc(dve_evac, 1)

            dve.wait_ge(x_in, 16 * (NT + 1))
            dve.wait_ge(rstd_done, 1)
            for t in range(NT):
                nc.vector.tensor_scalar(xs[:, t, :], xs[:, t, :], stat[:, 8 + t:9 + t], None, ALU.mult)\
                    .then_inc(xn_done, 1)
            dve.wait_ge(rstd_done, 2)
            nc.vector.tensor_scalar(xmeta[0:META, :], xmeta[0:META, :], stat[0:META, 12:13], None, ALU.mult)\
                .then_inc(xn_done, 1)
            dve.wait_ge(small_in, SMALL)
            for c in range(1, KC, 2):
                wait_group(dve, f"hT{c}")
                freed(nc.vector.tensor_scalar(hT[:, c, META:L], bank(f"hT{c}"), gains[:, GN + c:GN + c + 1], None,
                                              ALU.mult), f"hT{c}")
            wait_group(dve, "hTm")
            freed(nc.vector.tensor_tensor(hT[:, :, 0:META], bank("hTm")[:, 0:P].rearrange("p (c m) -> p c m", c=KC),
                                          gains[:, GN:GN + KC].unsqueeze(2).to_broadcast([P, KC, META]), ALU.mult),
                  "hTm")
            for c in range(CH):
                dve.wait_ge(tanh_done, c + 1)
                freed(nc.vector.scalar_tensor_tensor(zp[:, c, :], zp[:, c, :], 1.0, bank(f"zp{c}"), ALU.add, ALU.mult),
                      f"zp{c}")
            wait_group(dve, "um")
            freed(nc.vector.tensor_copy(uT[:, :, 0:META], bank("um")[:, 0:CH * META]
                                        .rearrange("p (c m) -> p c m", c=CH)), "um")
            wait_group(dve, "km")
            freed(nc.vector.tensor_copy(kT[:, :, 0:META], bank("km")[:, 0:CH * META]
                                        .rearrange("p (c m) -> p c m", c=CH)), "km")
            wait_group(dve, "f")
            freed(nc.vector.tensor_scalar(lf[0:H, 0, META:L], bank("f")[0:H, :], gains[0:H, 40:41], None, ALU.add), "f")
            wait_group(dve, "fm")
            freed(nc.vector.tensor_scalar(lf[0:H, 0, 0:META], bank("fm")[0:H, 0:META], gains[0:H, 40:41], None,
                                          ALU.add), "fm")
            wait_evac(dve, "fm")
            dve.sem_inc(decay_x, 1)
            wait_evac(dve, "u3")
            wait_evac(dve, "um")
            for c in range(CH):
                src, left = uT[:, c, :], 0
                for s in range(c + 1):
                    step = 1 << s
                    dst = win[:, s % 2, :]
                    left += step
                    link(nc.vector.tensor_tensor(dst[:, left:L], src[:, left:L], src[:, left - step:L - step], ALU.add))
                    src = dst
                link(nc.vector.scalar_tensor_tensor(uT[:, c, META:L], src[:, META:L], 1.0 / (2 << c), uT[:, c, META:L],
                                                    ALU.mult, ALU.subtract))
                dve.sem_inc(pooled, 1)
            dve.wait_ge(decay_ln, 1)
            link(nc.vector.tensor_scalar(lf[0:H, 0, :], lf[0:H, 0, :], 0.0, None, ALU.min))
            nc.vector.tensor_tensor_scan(negc[:], lf[0:H, 1, :], lf[0:H, 0, :], 0.0, ALU.add, ALU.subtract)\
                .then_inc(decay_done, 1)
            link(nc.vector.tensor_scalar(gains[:, GP:GP + CH], gains[:, GP:GP + CH], 0.5, None, ALU.mult))
            wait_group(dve, "vm")
            freed(nc.vector.tensor_copy(vmeta[0:META, :], bank("vm")[0:META, :]), "vm")
            for c in range(CH):
                wait_group(dve, f"pm{c}")
                freed(nc.vector.scalar_tensor_tensor(zp[:, c, :], bank(f"pm{c}"), gains[:, GP + c:GP + c + 1],
                                                     zp[:, c, :], ALU.mult, ALU.mult), f"pm{c}")
            for c in range(CH):
                dve.wait_ge(tanh_done, CH + c + 1)
                freed(nc.vector.scalar_tensor_tensor(za[:, c, :], za[:, c, :], 1.0, bank(f"za{c}"), ALU.add, ALU.mult),
                      f"za{c}")
            wait_evac(dve, "za3")
            dve.sem_inc(pooled, 1)

            def normalise(n, i, buf, w, half, base):
                dve.wait_ge(exp_done, base + n + 1)
                link(nc.vector.reciprocal(stat[:, 104 + n % 4:105 + n % 4], stat[:, 100 + n % 4:101 + n % 4]))
                nc.vector.tensor_scalar(buf[:, n % 2, 0:w], buf[:, n % 2, 0:w], stat[:, 104 + n % 4:105 + n % 4],
                                        half, ALU.mult, ALU.mult).then_inc(norm_done, 1)

            def gated(n):
                i, h = ATT1[n]
                dve.wait_ge(pv_done, n + 1)
                cols = za[:, h // 2, i * P:(i + 1) * P]
                nc.vector.tensor_tensor(cols, psum[:, 6, 0:P], cols, ALU.mult).then_inc(y_done, 1)

            for n, (i, h) in enumerate(ATT1):
                w = (i + 1) * P + META
                dve.wait_ge(s_done, n + 1)
                s_ps = psum[:, 2 * (n % 2):2 * (n % 2) + 2, :].rearrange("p a b -> p (a b)")
                if n >= 4:
                    dve.wait_ge(norm_done, n - 3)
                nc.vector.tensor_reduce(stat[:, 96 + n % 4:97 + n % 4], s_ps[:, 0:w], AX, ALU.max, negate=True)\
                    .then_inc(max_done, 1)
                if n:
                    pi = ATT1[n - 1][0]
                    normalise(n - 1, pi, Pb, (pi + 1) * P + META, 0.5, 0)
                if n >= 4 and n % 2 == 0:
                    gated(n - 3)
            normalise(N1 - 1, NT - 1, Pb, L, 0.5, 0)
            gated(N1 - 3)
            gated(N1 - 1)

            for c in range(KC):
                for s in range(2):
                    wait_group(dve, f"up{s}{c}")
                    if s == 0 and c == 0:
                        wait_evac(dve, "g17")
                    freed(nc.vector.scalar_tensor_tensor(gate[:, s, c, :], gate[:, s, c, :], 1.0, bank(f"up{s}{c}"),
                                                         ALU.add, ALU.mult), f"up{s}{c}")
                wait_evac(dve, f"up1{c}")
                nc.vector.tensor_tensor(gate[:, 0, c, :], gate[:, 0, c, :], gate[:, 1, c, :], ALU.add)\
                    .then_inc(merged_done, 1)
            dve.wait_ge(xres_in, 16 * NT)

            def x2T_evac(t):
                for j in range(2):
                    wait_group(dve, f"x2T{t}{j}")
                    freed(nc.vector.tensor_tensor(x2T[:, 4 * j:4 * j + 4, t * P:(t + 1) * P],
                                                  bank(f"x2T{t}{j}").rearrange("p (c t) -> p c t", c=4),
                                                  gains[:, GA2 + 4 * j:GA2 + 4 * j + 4].unsqueeze(2)
                                                  .to_broadcast([P, 4, P]), ALU.mult), f"x2T{t}{j}")

            for t in range(NT):
                for e in range(2):
                    wait_group(dve, f"y{t}{e}")
                    freed(nc.vector.scalar_tensor_tensor(x1[:, t, 512 * e:512 * e + 512], bank(f"y{t}{e}"), 0.5,
                                                         x1[:, t, 512 * e:512 * e + 512], ALU.mult, ALU.add),
                          f"y{t}{e}")
                wait_evac(dve, f"y{t}1")
                dve.sem_inc(x1_done, 1)
                dve.wait_ge(rstd_done, 2 + 2 * t + 1)
                nc.vector.scalar_tensor_tensor(x1[:, t, :], x1[:, t, :], stat[:, 20 + t:21 + t], gain_row[:],
                                               ALU.mult, ALU.mult).then_inc(x1_done, 1)
                dve.wait_ge(x1_done, 2 * t + 2)
                dve.wait_ge(rstd_done, 2 + 2 * t + 2)
                if t >= 2:
                    wait_group(dve, f"x2T{t - 2}1")
                nc.vector.tensor_scalar(xn2[:, t % 2, :], x1[:, t, :], stat[:, 28 + t:29 + t], None, ALU.mult)\
                    .then_inc(xn_done, 1)
                if t:
                    x2T_evac(t - 1)
            x2T_evac(NT - 1)

            dve.wait_ge(consts, 1)
            link(nc.vector.tensor_copy(posf[:], posi[:]))
            for t in range(NT):
                link(nc.vector.tensor_scalar(trig[:, 1, t, :], freq[:], posf[:, t:t + 1], None, ALU.mult))
            turns = 1 / TWO_PI
            ang = trig[:, 1].rearrange("p t r -> p (t r)")
            for q in range(2):
                link(nc.vector.tensor_scalar(angle[:, q, :], ang, turns, 0.25 * (1 - q), ALU.mult, ALU.add))
                link(nc.vector.tensor_scalar(angle[:, q, :], angle[:, q, :], MAGIC, -MAGIC, ALU.add, ALU.add))
            for q in range(2):
                r = trig[:, q].rearrange("p t r -> p (t r)")
                src = ang
                for part in (TP1, TP2, TP3):
                    link(nc.vector.scalar_tensor_tensor(r, angle[:, q, :], -part, src, ALU.mult, ALU.add))
                    src = r
                if q == 0:
                    link(nc.vector.tensor_scalar(r, r, float(np.pi / 2), None, ALU.add))
                link(nc.vector.tensor_scalar(r, r, 3.1415925, -3.1415925, ALU.min, ALU.max))
            dve.sem_inc(rope_arg, 1)

            for t in range(NT):
                dve.wait_ge(rstd_done, 2 + 2 * NT + 2 * t + 2)
                nc.vector.tensor_scalar(cqt[:, t, 0:CQ], cqt[:, t, 0:CQ], stat[:, 40 + t:41 + t], None, ALU.mult)\
                    .then_inc(xn_done, 1)
                nc.vector.tensor_scalar(cqt[:, t, CQ:CQ + CKV], cqt[:, t, CQ:CQ + CKV], stat[:, 44 + t:45 + t], None,
                                        ALU.mult).then_inc(xn_done, 1)
            def latents(t):
                for tag, n, c0, g in ((f"cqT{t}", 3, 0, GC), (f"ckvT{t}", 2, 3, GKV)):
                    wait_group(dve, tag)
                    c0 += 5 * (t % 2)
                    freed(nc.vector.tensor_tensor(latT[:, c0:c0 + n, :],
                                                  bank(tag)[:, 0:n * P].rearrange("p (c t) -> p c t", c=n),
                                                  gains[:, g:g + n].unsqueeze(2).to_broadcast([P, n, P]), ALU.mult),
                          tag)
            latents(0)
            dve.wait_ge(trig_done, 1)
            R2 = ROPE // 2
            for t in range(NT):
                if t + 1 < NT:
                    latents(t + 1)
                dve.wait_ge(rows_squared, 2 * t + 2)
                for j in range(2):
                    nc.vector.tensor_reduce(stat[:, 48 + 8 * j:56 + 8 * j], rsq[:, j], AX, ALU.add).then_inc(row_sq, 1)
                dve.wait_ge(rstd_done, 2 + 4 * NT + t + 1)
                for j in range(2):
                    r = rows[:, j]
                    link(nc.vector.tensor_tensor(r, r, stat[:, 64 + 8 * j:72 + 8 * j].unsqueeze(2)
                                                 .to_broadcast([P, H, QK]), ALU.mult))
                    link(nc.vector.tensor_tensor(r, r, qk_gain[:, j, :].unsqueeze(1).to_broadcast([P, H, QK]),
                                                 ALU.mult))
                    a1, a2 = r[:, :, HD:HD + R2], r[:, :, HD + R2:QK]
                    cos = trig[:, 0, t, :].unsqueeze(1).to_broadcast([P, H, R2])
                    sin = trig[:, 1, t, :].unsqueeze(1).to_broadcast([P, H, R2])
                    tm = [rtmp[:, q, 0:H * R2].rearrange("p (h r) -> p h r", h=H) for q in range(4)]
                    nc.vector.tensor_tensor(tm[0], a1, cos, ALU.mult)
                    nc.vector.tensor_tensor(tm[1], a2, sin, ALU.mult)
                    nc.vector.tensor_tensor(tm[2], a1, sin, ALU.mult)
                    link(nc.vector.tensor_tensor(tm[3], a2, cos, ALU.mult))
                    nc.vector.tensor_tensor(a1, tm[0], tm[1], ALU.subtract)
                    link(nc.vector.tensor_tensor(a2, tm[2], tm[3], ALU.add))
                    dve.sem_inc(rope_done, 1)

            def outputs(m):
                i, kind, h = ATT2[m]
                dve.wait_ge(osq_done, m // 2 + 1)
                c = CH * kind + h // 2
                nc.vector.tensor_scalar(og[:, c, i * P:(i + 1) * P], psum[:, 6, 0:P],
                                        gains[:, GSB + c:GSB + c + 1], None, ALU.mult).then_inc(og_done, 1)

            def combine(i):
                dve.wait_ge(oss_done, 8 * (i + 1))
                nc.vector.tensor_copy(stat[:, 80:82], psum[:, 7, 0:2]).then_inc(oms_done, 1)
                dve.wait_ge(orstd_done, i + 1)
                for e in range(2):
                    dve.wait_ge(wo_done, 2 * i + e + 1)
                    cols = x1[:, i, 512 * e:512 * e + 512]
                    for kind in range(2):
                        link(nc.vector.scalar_tensor_tensor(cols, psum[:, 1 + 2 * kind, :], stat[:, 82 + kind:83 + kind],
                                                            cols, ALU.mult, ALU.add))
                    dve.sem_inc(x2_half, 1)
                dve.sem_inc(x2_done, 1)

            sb_n = ml_n = 0
            for m, (i, kind, h) in enumerate(ATT2):
                w = (i + 1) * P
                s_ps = psum[:, 2 * (m % 2), 0:w]
                dve.wait_ge(s_done, N1 + m + 1)
                if kind == 0:
                    sb_n += 1
                    if sb_n > 1:
                        dve.wait_ge(exp_done, N1 + m - (8 if h == 0 else 0))
                    dve.wait_ge(z_abs, sb_n)
                    link(nc.vector.tensor_scalar(st[:, 1, 0:w], s_ps, 0.0, None, ALU.max))
                    dve.wait_ge(sp_done, sb_n)
                    link(nc.vector.tensor_tensor_scan(st[:, 2, w - 1::-1], st[:, 0, w - 1::-1], st[:, 1, w - 1::-1],
                                                      0.0, ALU.add, ALU.add))
                    nc.vector.tensor_tensor(st[:, 1, 0:w], s_ps, st[:, 2, 0:w], ALU.subtract).then_inc(zr_done, 1)
                else:
                    ml_n += 1
                    link(nc.vector.tensor_reduce(stat[:, 108:109], s_ps, AX, ALU.max, negate=True))
                    nc.vector.tensor_scalar(stat[:, 96 + m % 4:97 + m % 4], stat[:, 108:109], QK ** -0.5, None,
                                            ALU.mult).then_inc(max_done, 1)
                    normalise(m, i, Pb2, w, 1.0, N1)
                if m >= 2 and m % 2 == 1:
                    outputs(m - 2)
                if m % 16 == 1 and m > 16:
                    combine(m // 16 - 1)
            outputs(N2 - 1)
            combine(NT - 1)

            chain = [0]

            def prep_norm(t):
                if t == 0:
                    dve.wait_ge(p_rstd, 1)
                    dve.wait_ge(grow_in, 16)
                if t >= 2:
                    dve.wait_ge(u_used, H * TOPK * (t - 1))
                nc.vector.scalar_tensor_tensor(xn[:, t % 2, :], x1[:, t, :], stat[:, 88 + t:89 + t], gain_row[:],
                                               ALU.mult, ALU.mult).then_inc(p_xn, 1)

            def top16(values, spare, tops_ap, index_ap):
                link(nc.vector.max(tops_ap[:, 0:8], values))
                nc.vector.max_index(index_ap[:, 0:8], tops_ap[:, 0:8], values)
                link(nc.vector.match_replace(spare, tops_ap[:, 0:8], values, BELOW))
                link(nc.vector.max(tops_ap[:, 8:16], spare))
                link(nc.vector.max_index(index_ap[:, 8:16], tops_ap[:, 8:16], spare))

            def prep_top(t, h):
                g = [n for n, p in enumerate(PREP) if p == ("s", h // 4)][0]
                g2 = [n for n, p in enumerate(PREP) if p == ("s", 2 + h // 4)][0]
                dve.wait_ge(prep_evac, SUBK_GROUPS + len(PREP) * t + max(g, g2) + 1)
                for half in range(2):
                    hc = H * half + h
                    top16(sc[:, hc, :], sc2[:, 0:P], tops[:, hc, :], topi[:, hc, :])
                link(nc.vector.tensor_tensor(cand.rearrange("p (a b) -> p a b", a=TOPK),
                                             tops[:, h, :].unsqueeze(2).to_broadcast([P, TOPK, TOPK]),
                                             tops[:, H + h, :].unsqueeze(1).to_broadcast([P, TOPK, TOPK]), ALU.add))
                top16(cand[:], cand2[:], best[:, h, :], posn[:, h, :])

            def prep_index(t):
                nc.vector.tensor_scalar(posab[:, 0, :], posn[:].rearrange("p h k -> p (h k)"), 4, None,
                                        ALU.logical_shift_right)
                nc.vector.tensor_scalar(posab[:, 1, :], posn[:].rearrange("p h k -> p (h k)"), TOPK - 1, None,
                                        ALU.bitwise_and)
                link(nc.vector.tensor_copy(topif[:], topi[:]))
                link(nc.vector.tensor_copy(posf2[:], posab[:]))
                for half in range(2):
                    oh = onehot.rearrange("p (h k) a -> p h k a", h=H)
                    link(nc.vector.tensor_tensor(onehot[:], posf2[:, half, :].unsqueeze(2)
                                                 .to_broadcast([P, H * TOPK, TOPK]),
                                                 iota[:].unsqueeze(1).to_broadcast([P, H * TOPK, TOPK]), ALU.is_equal))
                    link(nc.vector.tensor_tensor(oh, oh, topif[:, H * half:H * half + H, :].unsqueeze(2)
                                                 .to_broadcast([P, H, TOPK, TOPK]), ALU.mult))
                    link(nc.vector.tensor_reduce(idxf[:, half, :], onehot[:], AX, ALU.add))
                link(nc.vector.scalar_tensor_tensor(idxf[:, 2, :], idxf[:, 0, :], float(NK), idxf[:, 1, :], ALU.mult,
                                                    ALU.add))
                if t >= 2:
                    dve.wait_ge(v_used, H * TOPK * (t - 1))
                nc.vector.tensor_copy(idx[:, t % 2, :], idxf[:, 2, :]).then_inc(idx_ready, 1)
                sv_ = soft[:, t % 2, :].rearrange("p (h k) -> p h k", h=H)
                nc.vector.tensor_tensor(sv_, best[:], best[:, :, 0:1].to_broadcast([P, H, TOPK]), ALU.subtract)\
                    .then_inc(soft_in, 1)

            def prep_soft(t):
                dve.wait_ge(soft_exp, t + 1)
                sv_ = soft[:, t % 2, :].rearrange("p (h k) -> p h k", h=H)
                link(nc.vector.tensor_reduce(stat[:, 110:118], sv_, AX, ALU.add))
                link(nc.vector.reciprocal(stat[:, 118:126], stat[:, 110:118]))
                link(nc.vector.tensor_tensor(sv_, sv_, stat[:, 118:126].unsqueeze(2).to_broadcast([P, H, TOPK]),
                                             ALU.mult))

            prep_norm(0)
            for h in range(H):
                prep_top(0, h)
            prep_index(0)
            prep_soft(0)

            def dots(t, c):
                for s in range(c * TOPK, (c + 1) * TOPK):
                    g = u_gather(t, s)
                    if s % TOPK == 4 and (t or c):
                        weigh(*divmod(H * t + c - 1, H))
                    dve.wait_ge(landed[g % NB], 16 * (g // NB + 1))
                    if t and s % TOPK == 0:
                        dve.wait_ge(gelu_done, H * (t - 1) + c + 1)
                    nc.vector.tensor_tensor_reduce(out=gbuf[:, g % NB, :], in0=gbuf[:, g % NB, :],
                                                   in1=xn[:, t % 2, :], scale=1.0, scalar=0.0, op0=ALU.mult,
                                                   op1=ALU.add, accum_out=pre[:, s:s + 1]).then_inc(u_used, 1)

            def weigh(t, c):
                dve.wait_ge(gelu_done, H * t + c + 1)
                cols = slice(c * TOPK, (c + 1) * TOPK)
                if t:
                    dve.wait_ge(diag_done, H * TOPK * (t - 1) + (c + 1) * TOPK)
                nc.vector.tensor_tensor(coef[:, cols], gel[:, cols], soft[:, t % 2, cols], ALU.mult)\
                    .then_inc(coef_done, 1)

            def finish(t):
                dve.wait_ge(acc_done, t + 1)
                if t:
                    dve.wait_ge(out_sent, 16 * t)
                nc.vector.tensor_tensor(ostage[:], x1[:, t, :], psum[:, 0:2, :].rearrange("p a b -> p (a b)"),
                                        ALU.add).then_inc(acc_read, 1)

            dots(0, 0)
            for t in range(NT):
                for c in range(H):
                    if c == 0 and t:
                        finish(t - 1)
                    if c == 0 and t + 1 < NT:
                        prep_norm(t + 1)
                    if t + 1 < NT:
                        for h in TOP_AT[c]:
                            prep_top(t + 1, h)
                        if c == SOFT_AT:
                            prep_index(t + 1)
                            prep_soft(t + 1)
                    if c + 1 < H:
                        dots(t, c + 1)
                    elif t + 1 < NT:
                        dots(t + 1, 0)
            weigh(NT - 1, H - 1)
            finish(NT - 1)

        @block.tensor
        def _(pe):
            def mm(o, l, r, start, stop):
                return nc.tensor.matmul(o, l, r, start=start, stop=stop)

            def finished(ins):
                ins.then_inc(dense_done, 1)

            pe.wait_ge(consts, 1)
            pe.wait_ge(xn_done, NT)
            for c in range(KC):
                wait_bank(pe, f"hT{c}")
                for t in range(NT):
                    last = nc.tensor.transpose(bank(f"hT{c}")[:, t * P:(t + 1) * P], xs[:, t, c * P:(c + 1) * P],
                                               ident[:])
                finished(last)
            pe.wait_ge(xn_done, NT + 1)
            wait_bank(pe, "hTm")
            for c in range(KC):
                last = nc.tensor.transpose(bank("hTm")[:, c * META:(c + 1) * META], xmeta[0:META, c * P:(c + 1) * P],
                                           ident[0:META, 0:META])
            finished(last)
            for tag in ("hT6", "hT7", "hTm"):
                wait_evac(pe, tag)

            def feature_major(name, meta=None):
                wait_weights(pe, name)
                w = weights(name)
                for c in range(CH):
                    tag = f"{name}{c}"
                    wait_bank(pe, tag)
                    for k in range(KC):
                        last = mm(bank(tag), w[:, k, c * P:(c + 1) * P], hT[:, k, META:L], k == 0, k == KC - 1)
                    finished(last)
                if meta:
                    wait_bank(pe, meta)
                    for c in range(CH):
                        for k in range(KC):
                            last = mm(bank(meta)[:, c * META:(c + 1) * META], w[:, k, c * P:(c + 1) * P],
                                      hT[:, k, 0:META], k == 0, k == KC - 1)
                    finished(last)

            feature_major("zp")
            feature_major("u", "um")
            feature_major("k", "km")
            pe.wait_ge(small_in, SMALL)
            wait_bank(pe, "f")
            for k in range(KC):
                last = mm(bank("f")[0:H, :], f_w[:, k, :], hT[:, k, META:L], k == 0, k == KC - 1)
            finished(last)
            wait_bank(pe, "fm")
            for k in range(KC):
                last = mm(bank("fm")[0:H, 0:META], f_w[:, k, :], hT[:, k, 0:META], k == 0, k == KC - 1)
            finished(last)
            feature_major("q")
            wait_weights(pe, "v")
            for t in range(NT):
                wait_bank(pe, f"v{t}")
                for k in range(KC):
                    last = mm(bank(f"v{t}"), hT[:, k, META + t * P:META + (t + 1) * P], weights("v")[:, k, :],
                              k == 0, k == KC - 1)
                finished(last)
            wait_bank(pe, "vm")
            for k in range(KC):
                last = mm(bank("vm")[0:META, :], hT[:, k, 0:META], weights("v")[:, k, :], k == 0, k == KC - 1)
            finished(last)
            for c in range(CH):
                pe.wait_ge(pooled, c + 1)
                wait_bank(pe, f"pm{c}")
                finished(mm(bank(f"pm{c}"), poolw[:, c, :], uT[:, c, META:L], True, True))
            feature_major("za")

            for by in "AV":
                pe.wait_ge(evac_sem[by], sum(b == by for _, b in plan[:before_attention]))
            pe.wait_ge(decay_done, 1)

            def scores1(n):
                i, h = ATT1[n]
                if n >= 2:
                    pe.wait_ge(exp_done, n - 1)
                    if ATT1[n - 2][0] == NT - 1:
                        pe.wait_ge(pT_copied, n - 1)
                b, lo = 2 * (n % 2), HD * (h % 2)
                q = qT[lo:lo + HD, h // 2, i * P:(i + 1) * P]
                w = (i + 1) * P
                mb, mc = (b, w) if i < NT - 1 else (b + 1, 0)
                for o, k0, k1 in ((psum[:, b, 0:w], META, META + w), (psum[:, mb, mc:mc + META], 0, META)):
                    mm(o, q, kT[lo:lo + HD, h // 2, k0:k1], True, False)
                    last = mm(o, sel8[:, h, :], negc[:, k0:k1], False, k0 == 0)
                    if k0:
                        last = mm(o[:, i * P:w], identb[:], masks[:, 0, :], False, True)
                last.then_inc(s_done, 1)

            def transposes1(n):
                i, h = ATT1[n]
                pe.wait_ge(norm_done, n + 1)
                if n >= 2:
                    pe.wait_ge(pT_copied, n - 1)
                for j in range(i + 1):
                    nc.tensor.transpose(psum[:, 4 + n % 2, j * P:(j + 1) * P], Pb[:, n % 2, j * P:(j + 1) * P],
                                        ident[:])
                nc.tensor.transpose(meta_ps(n, i), Pb[:, n % 2, (i + 1) * P:(i + 1) * P + META], ident[:])\
                    .then_inc(pT_done, 1)

            def values1(n):
                i, h = ATT1[n]
                pe.wait_ge(pT_copied, n + 1)
                if n % 2 == 0 and n:
                    pe.wait_ge(y_done, n // 2)
                o = psum[HD * (h % 2):HD * (h % 2) + HD, 6, 0:P]
                hc = slice(h * HD, (h + 1) * HD)
                mm(o, vmeta[0:META, hc], PT[0:META, n % 2, 4, :], True, False)
                for j in range(i + 1):
                    last = mm(o, vtok[:, j, hc], PT[:, n % 2, j, :], False, j == i)
                last.then_inc(pv_done, 1)

            scores1(0)
            for n in range(N1):
                if n + 1 < N1:
                    scores1(n + 1)
                s, c = GATES[n // 2]
                tag = f"g{s}{c}"
                name = f"g{s}{c // 4}"
                if n % 2 == 0:
                    wait_weights(pe, name)
                    wait_bank(pe, tag)
                for k in range(4 * (n % 2), 4 * (n % 2) + 4):
                    last = mm(bank(tag), weights(name)[:, k, (c % 4) * P:(c % 4 + 1) * P], hT[:, k, META:L], k == 0,
                              k == KC - 1)
                if n % 2:
                    finished(last)
                transposes1(n)
                if n:
                    values1(n - 1)
            values1(N1 - 1)

            pe.wait_ge(exp_done, N1)
            pe.wait_ge(pT_copied, N1)
            pe.wait_ge(y_done, N1 // 2)
            for c in range(KC):
                for s, (name, y) in enumerate((("wup0", zp), ("wup1", za))):
                    wait_weights(pe, name)
                    wait_bank(pe, f"up{s}{c}")
                    for k in range(CH):
                        last = mm(bank(f"up{s}{c}"), weights(name)[:, k, c * P:(c + 1) * P], y[:, k, :], k == 0,
                                  k == CH - 1)
                    finished(last)
            def transposed_rows(t):
                pe.wait_ge(xn_done, NT + 1 + t + 1)
                for j in range(2):
                    tag = f"x2T{t}{j}"
                    wait_bank(pe, tag)
                    for c in range(4):
                        last = nc.tensor.transpose(bank(tag)[:, c * P:(c + 1) * P],
                                                   xn2[:, t % 2, (4 * j + c) * P:(4 * j + c + 1) * P], ident[:])
                    finished(last)

            for t in range(NT):
                for e in range(2):
                    wait_bank(pe, f"y{t}{e}")
                    for k in range(KC):
                        pe.wait_ge(merged_done, k + 1)
                        wait_weights(pe, f"wout{k // 4}")
                        last = mm(bank(f"y{t}{e}"), gate[:, 0, k, t * P:(t + 1) * P],
                                  weights(f"wout{k // 4}")[:, k % 4, 512 * e:512 * e + 512], k == 0, k == KC - 1)
                    finished(last)
                if t:
                    transposed_rows(t - 1)
            transposed_rows(NT - 1)

            wait_evac(pe, "x2T31")
            for name in ("sq", "sk"):
                wait_weights(pe, name)
                for c in range(CH):
                    wait_bank(pe, f"{name}{c}")
                    for k in range(KC):
                        last = mm(bank(f"{name}{c}"), weights(name)[:, k, c * P:(c + 1) * P], x2T[:, k, :], k == 0,
                                  k == KC - 1)
                    finished(last)

            def token_major(tag, name, t, c0, c1):
                wait_weights(pe, name)
                wait_bank(pe, tag)
                for k in range(KC):
                    last = mm(bank(tag)[:, 0:c1 - c0], x2T[:, k, t * P:(t + 1) * P], weights(name)[:, k, c0:c1],
                              k == 0, k == KC - 1)
                finished(last)

            for t in range(NT):
                token_major(f"sv{t}", "sv", t, 0, 512)
            for t in range(NT):
                token_major(f"cq{t}", "cq", t, 0, CQ)
                token_major(f"ckv{t}", "ckv", t, 0, CKV + ROPE)
            def latents(t):
                pe.wait_ge(xn_done, 2 * NT + 1 + 2 * t + 2)
                for tag, n, c0 in ((f"cqT{t}", 3, 0), (f"ckvT{t}", 2, CQ)):
                    wait_bank(pe, tag)
                    for c in range(n):
                        last = nc.tensor.transpose(bank(tag)[:, c * P:(c + 1) * P],
                                                   cqt[:, t, c0 + c * P:c0 + (c + 1) * P], ident[:])
                    finished(last)
            latents(0)
            for t in range(NT):
                wait_evac(pe, f"ckvT{t}")
                for base, n, name, w in (("uq", 3, "uq", 4 * QK), ("ukv", 2, "ukv", 512)):
                    wait_weights(pe, name)
                    for j in range(2):
                        tag = f"{base}{t}{j}"
                        wait_bank(pe, tag)
                        for k in range(n):
                            last = mm(bank(tag)[:, 0:w], latT[:, 5 * (t % 2) + (k if n == 3 else 3 + k), :],
                                      weights(name)[:, k, j * w:(j + 1) * w], k == 0, k == n - 1)
                        finished(last)
                if t + 1 < NT:
                    latents(t + 1)
                for j in range(2):
                    pe.wait_ge(rope_done, 2 * t + j + 1)
                    for g in range(2):
                        tag = f"qkT{t}{j}{g}"
                        wait_bank(pe, tag)
                        for h in range(4):
                            last = nc.tensor.transpose(bank(tag)[0:QK, h * P:(h + 1) * P], rows[:, j, 4 * g + h, :],
                                                       ident[:])
                        finished(last)

            pe.wait_ge(act_evac, all_dense_a)
            pe.wait_ge(dve_evac, all_dense_v)

            def scores2(m):
                i, kind, h = ATT2[m]
                if m >= 2:
                    pe.wait_ge(exp_done, N1 + m - 1)
                o = psum[:, 2 * (m % 2), 0:(i + 1) * P]
                if kind == 0:
                    lo = HD * (h % 2)
                    mm(o, sq[lo:lo + HD, h // 2, i * P:(i + 1) * P], sk[lo:lo + HD, h // 2, 0:(i + 1) * P], True, False)
                else:
                    mm(o, mq[0:QK, h, i * P:(i + 1) * P], mk[0:QK, h, 0:(i + 1) * P], True, False)
                mm(o[:, i * P:(i + 1) * P], identb[:], masks[:, 1 + kind, :], False, True).then_inc(s_done, 1)

            def transposes2(m):
                i, kind, h = ATT2[m]
                if kind == 0:
                    pe.wait_ge(exp_done, N1 + m + 1)
                else:
                    pe.wait_ge(norm_done, N1 + ml_count(m))
                if m >= 2:
                    pe.wait_ge(pT_copied, N1 + m - 1)
                for j in range(i + 1):
                    last = nc.tensor.transpose(psum[:, 4 + m % 2, j * P:(j + 1) * P],
                                               Pb2[:, m % 2, j * P:(j + 1) * P], ident[:])
                last.then_inc(pT_done, 1)

            def values2(m):
                i, kind, h = ATT2[m]
                pe.wait_ge(pT_copied, N1 + m + 1)
                if m % 2 == 0 and m:
                    pe.wait_ge(osq_done, m // 2)
                    pe.wait_ge(og_done, m // 2)
                o = psum[HD * (h % 2):HD * (h % 2) + HD, 6, 0:P]
                v = (sv, mv)[kind]
                for j in range(i + 1):
                    last = mm(o, v[:, j, h * HD:(h + 1) * HD], PT2[:, m % 2, j, :], j == 0, j == i)
                last.then_inc(pv_done, 1)

            def sums(m):
                i, kind, h = ATT2[m]
                pe.wait_ge(osq_done, m // 2 + 1)
                if m % 16 == 1 and i:
                    pe.wait_ge(oms_done, i)
                mm(psum[:, 7, kind:kind + 1], osq[:, (m // 2) % 2, :], ones[:], h == 1, h == H - 1)\
                    .then_inc(oss_done, 1)

            def project(i):
                for e in range(2):
                    if i or e:
                        pe.wait_ge(x2_half, 2 * i + e)
                    for kind in range(2):
                        wait_weights(pe, f"wo{kind}")
                        for k in range(CH):
                            if k == 0:
                                pe.wait_ge(og_done, 8 * (i + 1))
                            last = mm(psum[:, 1 + 2 * kind, :], og[:, CH * kind + k, i * P:(i + 1) * P],
                                      weights(f"wo{kind}")[:, k, 512 * e:512 * e + 512], k == 0, k == CH - 1)
                    last.then_inc(wo_done, 1)

            scores2(0)
            for m in range(N2):
                if m + 1 < N2:
                    scores2(m + 1)
                transposes2(m)
                if m:
                    values2(m - 1)
                if m >= 3 and m % 2 == 1:
                    sums(m - 2)
                if m % 16 == 1 and m > 16:
                    project(m // 16 - 1)
            values2(N2 - 1)
            sums(N2 - 1)
            project(NT - 1)

            pe.wait_ge(x2_done, NT)
            def prep_bank(n):
                if n >= 4:
                    pe.wait_ge(prep_evac, n - 3)

            wait_weights(pe, "subk")
            for j in range(SUBK_GROUPS):
                prep_bank(j)
                for c in range(4):
                    last = nc.tensor.transpose(psum[:, 4 + j % 4, c * P:(c + 1) * P],
                                               weights("subk")[:, 4 * j + c, :], ident[:])
                last.then_inc(prep_mm, 1)

            def prepare(t, n):
                kind, j = PREP[n]
                g = SUBK_GROUPS + len(PREP) * t + n
                prep_bank(g)
                o = psum[:, 4 + g % 4, :]
                base = SUBK_GROUPS + len(PREP) * t
                if kind == "xT":
                    pe.wait_ge(p_xn, t + 1)
                    for c in range(4):
                        last = nc.tensor.transpose(o[:, c * P:(c + 1) * P],
                                                   xn[:, t % 2, (4 * j + c) * P:(4 * j + c + 1) * P], ident[:])
                elif kind == "q":
                    pe.wait_ge(prep_evac, base + 2)
                    wait_weights(pe, f"pq{j}")
                    for c in range(4):
                        for k in range(KC):
                            last = mm(o[:, c * P:(c + 1) * P], weights(f"pq{j}")[:, k, c * P:(c + 1) * P],
                                      xnT[:, k, :], k == 0, k == KC - 1)
                else:
                    pe.wait_ge(prep_evac, base + 6)
                    half = j // 2
                    for c in range(4):
                        h = 4 * (j % 2) + c
                        last = mm(o[:, c * P:(c + 1) * P], pq[:, 2 * h + half, :], skT[:, H * half + h, :], True, True)
                last.then_inc(prep_mm, 1)

            for n in range(len(PREP)):
                prepare(0, n)

            def weighted(t, c):
                for s in range(c * TOPK, (c + 1) * TOPK):
                    g = v_gather(t, s)
                    n = H * TOPK * t + s
                    if s == 0 and t:
                        pe.wait_ge(acc_read, t)
                    pe.wait_ge(diag_done, n + 1)
                    pe.wait_ge(landed[g % NB], 16 * (g // NB + 1))
                    for e in range(2):
                        last = mm(psum[:, e, :], diag[:, n % 4, :], gbuf[:, g % NB, 512 * e:512 * e + 512], s == 0,
                                  s == H * TOPK - 1)
                    last.then_inc(v_used, 1)
                    if s == H * TOPK - 1:
                        pe.wait_ge(v_used, n + 1)
                        pe.sem_inc(acc_done, 1)

            for t in range(NT):
                for c in range(H):
                    weighted(t, c)
                    if t + 1 < NT:
                        for n in PREP_AT[c]:
                            prepare(t + 1, n)



def kernel(**inputs):
    import numpy as _np
    import concourse.bacc as _bacc
    from concourse import mybir as _mybir
    from concourse.bass_utils import run_bass_kernel_spmd as _run

    nc = _bacc.Bacc("TRN2", target_bir_lowering=False, num_devices=1)
    arrays, aps = {}, {}
    for name, value in inputs.items():
        v = _np.ascontiguousarray(value)
        arrays[f"in_{name}"] = v
        aps[name] = nc.dram_tensor(f"in_{name}", v.shape, _mybir.dt.from_np(v.dtype), kind="ExternalInput").ap()
    out = nc.dram_tensor("out_0", (1, T, D), F32, kind="ExternalOutput").ap()
    build(nc, aps, out)
    return _run(nc, [arrays], core_ids=[0]).results[0]["out_0"]
```

```python
from contextlib import ExitStack

import numpy as np

import concourse.bass as bass
from concourse import mybir

ALU = mybir.AluOpType
ACT = mybir.ActivationFunctionType
F32 = mybir.dt.float32
BF16 = mybir.dt.bfloat16
U32 = mybir.dt.uint32
I32 = mybir.dt.int32
AX = mybir.AxisListType.X

P = 128
D = 1024
T = 512
NT = T // P
META = 16
L = META + T
KC = D // P
H = 8
HD = 64
CH = T // P
EPS = 1e-6
NEG = -1e30
BELOW = -3e38

CQ, CKV, ROPE = 384, 256, 32
QK = 96
NK = 128
TOPK = 16
SLOTS = 5
SW = 4096
INV_FREQ = 1.0 / (np.float32(10000.0) ** (np.arange(ROPE // 2, dtype=np.float32) * np.float32(2.0 / ROPE)))
TWO_PI = 2 * np.pi
TP1 = 6.28125
TP2 = float(np.float32(np.round((TWO_PI - TP1) * 2**21) / 2**21))
TP3 = float(np.float32(TWO_PI - TP1 - TP2))
MAGIC = 1.5 * 2**23


def build(nc, a, out):
    ctx = ExitStack()
    with ctx:
        def sb(name, shape, dt=F32):
            return ctx.enter_context(nc.sbuf_tensor("sb_" + name, shape, dt))

        def sem(name):
            return ctx.enter_context(nc.semaphore(name))

        wring = sb("wring", [P, SLOTS, SW])
        ident = sb("ident", [P, P])
        identb = sb("identb", [P, P], BF16)
        masks = sb("masks", [P, 3, P], BF16)
        ones = sb("ones", [P, 1])
        neg_half = sb("neg_half", [P, 2 * H])
        sel8 = sb("sel8", [H, H, P])
        gains = sb("gains", [P, 64])
        gain_row = sb("gain_row", [P, D])
        qk_gain = sb("qk_gain", [P, 2, QK])
        stat = sb("stat", [P, 128])
        negc = sb("negc", [H, L])
        freq = sb("freq", [P, ROPE // 2])
        trig = sb("trig", [P, 2, NT, ROPE // 2])
        posi = sb("posi", [P, NT], I32)
        posf = sb("posf", [P, NT])
        idx = sb("idx", [P, 2, H * TOPK], U32)
        iota = sb("iota", [P, TOPK])
        angle = sb("angle", [P, 2, NT * ROPE // 2])
        AW = nc.sbuf_bytes_remaining // 4 - 16
        arena = sb("arena", [P, AW])
        psum = ctx.enter_context(nc.psum_tensor("ps", [P, 8, 512], F32))

        def cut(at, *shape):
            n = int(np.prod(shape))
            assert at + n <= AW, (at, n, AW)
            v = arena[:, at:at + n]
            if len(shape) == 2:
                v = v.rearrange("p (a b) -> p a b", a=shape[0])
            elif len(shape) == 3:
                v = v.rearrange("p (a b c) -> p a b c", a=shape[0], b=shape[1])
            return v

        at = 0
        hT = cut(at, KC, L); at += KC * L
        qT = cut(at, CH, T); at += CH * T
        kT = cut(at, CH, L); at += CH * L
        vtok = cut(at, NT, T); at += NT * T
        vmeta = cut(at, T); at += T
        za = cut(at, CH, T); at += CH * T
        zp = cut(at, CH, T); at += CH * T
        gates_at = at
        gate = cut(at, 2, KC, T); at += 2 * KC * T
        Pb = cut(at, 2, L); at += 2 * L
        PT = cut(at, 2, 5, P); at += 2 * 5 * P
        xs = cut(gates_at, NT, D)
        xmeta = cut(gates_at + NT * D, D)
        uT = cut(gates_at, CH, L)
        win = cut(gates_at + CH * L, 2, L)
        lf = cut(gates_at + CH * L + 2 * L, 3, L)
        poolw = cut(gates_at + 6 * D, CH, P)
        f_w = cut(gates_at + 6 * D + CH * P, KC, H)
        junk = cut(gates_at + 7 * D, D)
        at2 = 0
        x1 = cut(at2, NT, D); at2 += NT * D
        hx = at2
        x2T = cut(at2, KC, T); at2 += KC * T
        sq = cut(at2, CH, T); at2 += CH * T
        sk = cut(at2, CH, T); at2 += CH * T
        mq = cut(at2, H, T); at2 += H * T
        mk = cut(at2, H, T); at2 += H * T
        sv = cut(at2, NT, T); at2 += NT * T
        mv = cut(at2, NT, T); at2 += NT * T
        scratch = at2
        xn2 = cut(scratch, 2, D)
        cqt = cut(scratch, NT, CQ + CKV + ROPE)
        latT = cut(scratch + NT * 672, 10, P)
        rows = cut(hx, 2, H, QK)
        rsq = cut(hx + 2 * H * QK, 2, H, QK)
        rtmp = cut(hx + 2 * H * QK, 4, H * (ROPE // 2))
        og = cut(hx, 2 * CH, T)
        Pb2 = cut(scratch, 2, T)
        PT2 = cut(scratch + 2 * T, 2, 4, P)
        soft_z = cut(scratch + 4 * T, 2, T)
        relu_z = cut(scratch + 6 * T, T)
        osq = cut(scratch + 7 * T, 2, 2, P)
        at3 = hx + 2 * CH * T
        xn = cut(at3, 2, D); at3 += 2 * D
        xnT = cut(at3, KC, P); at3 += KC * P
        pq = cut(at3, 2 * H, P); at3 += 2 * H * P
        skT = cut(at3, 2 * H, P); at3 += 2 * H * P
        sc = cut(at3, 2 * H, P); at3 += 2 * H * P
        spare2 = cut(at3, 2, P); at3 += 2 * P
        cand = cut(at3, 256)
        cand2 = cut(at3 + 256, 256)
        onehot = cut(at3, 2, TOPK, TOPK); at3 += 512
        tops = cut(at3, 2, TOPK); at3 += 2 * TOPK
        best = cut(at3, TOPK); at3 += TOPK
        topif = cut(at3, 2, TOPK); at3 += 2 * TOPK
        posf2 = cut(at3, 2, TOPK); at3 += 2 * TOPK
        idxf = cut(at3, 3, TOPK); at3 += 3 * TOPK
        topi = cut(at3, 2, TOPK).bitcast(U32); at3 += 2 * TOPK
        posn = cut(at3, TOPK).bitcast(U32); at3 += TOPK
        posab = cut(at3, 2, TOPK).bitcast(U32); at3 += 2 * TOPK
        soft = cut(at3, 2, H * TOPK); at3 += 2 * H * TOPK
        pre = cut(at3, H * TOPK); at3 += H * TOPK
        gel = cut(at3, H * TOPK); at3 += H * TOPK
        coef = cut(at3, H * TOPK); at3 += H * TOPK
        diag = cut(at3, 4, P); at3 += 4 * P
        gathered = [cut(at3 + n * D, D) for n in range((AW - at3) // D)]
        AFTER = len(gathered)
        gathered += [cut(hx + n * D, D) for n in range(3)]
        NB = len(gathered)
        ostage = cut(hx + 3 * D, D)

        rsq_junk = mk[:, 0, :]
        GN, GP, GA2, GC, GKV, GSB, GML = 0, 8, 12, 20, 23, 25, 29

        w_landed = [sem(f"w_landed{i}") for i in range(SLOTS)]
        x_in = sem("x_in"); small_in = sem("small_in"); xres_in = sem("xres_in"); grow_in = sem("grow_in")
        consts = sem("consts"); pool_chain = sem("pool_chain")
        dense_done = sem("dense_done"); act_evac = sem("act_evac"); dve_evac = sem("dve_evac")
        act_chain = sem("act_chain"); dve_chain = sem("dve_chain")
        ss_done = sem("ss_done"); rstd_done = sem("rstd_done"); ms_done = sem("ms_done")
        xn_done = sem("xn_done")
        tanh_done = sem("tanh_done"); pooled = sem("pooled"); decay_x = sem("decay_x")
        decay_ln = sem("decay_ln"); decay_done = sem("decay_done")
        s_done = sem("s_done"); max_done = sem("max_done"); exp_done = sem("exp_done")
        norm_done = sem("norm_done"); pT_done = sem("pT_done"); pT_copied = sem("pT_copied")
        pv_done = sem("pv_done"); y_done = sem("y_done")
        merged_done = sem("merged_done"); x1_done = sem("x1_done")
        rope_arg = sem("rope_arg"); trig_done = sem("trig_done")
        row_sq = sem("row_sq"); rows_squared = sem("rows_squared"); rope_done = sem("rope_done")
        osq_done = sem("osq_done"); og_done = sem("og_done"); oss_done = sem("oss_done")
        oms_done = sem("oms_done"); orstd_done = sem("orstd_done")
        s2_done = [sem("sb_scores"), sem("ml_scores")]; exp2_done = [sem("sb_exp"), sem("ml_exp")]
        ml_max = sem("ml_max"); ml_norm = sem("ml_norm")
        pT2_done = [sem("sb_pT"), sem("ml_pT")]; pT2_copied = [sem("sb_pT_copied"), sem("ml_pT_copied")]
        pv2_done = sem("pv2_done")
        z_abs = sem("z_abs"); sp_done = sem("sp_done"); zr_done = sem("zr_done")
        wo_done = sem("wo_done"); x2_added = sem("x2_added")
        p_ss = sem("p_ss"); p_rstd = sem("p_rstd"); p_xn = sem("p_xn"); prep_mm = sem("prep_mm")
        prep_evac = sem("prep_evac"); soft_in = sem("soft_in"); soft_exp = sem("soft_exp")
        idx_ready = sem("idx_ready"); top_done = sem("top_done")
        landed = [sem(f"gathered{i}") for i in range(NB)]
        u_used = sem("u_used"); v_used = sem("v_used"); gelu_done = sem("gelu_done")
        coef_done = sem("coef_done"); diag_done = sem("diag_done"); acc_done = sem("acc_done")
        acc_read = sem("acc_read"); out_sent = sem("out_sent")

        plan, index = [], {}

        def group(tag, bank, by):
            index[tag] = len(plan)
            plan.append((bank, by))

        turn = [0]

        def ring(tag, by, banks=8):
            group(tag, turn[0] % banks, by)
            turn[0] += 1

        evac_sem = {"A": act_evac, "V": dve_evac}

        def evac_count(tag):
            n = index[tag]
            by = plan[n][1]
            return evac_sem[by], sum(b == by for _, b in plan[:n + 1])

        def wait_evac(eng, tag):
            s, n = evac_count(tag)
            eng.wait_ge(s, n)

        def wait_group(eng, tag):
            eng.wait_ge(dense_done, index[tag] + 1)

        def bank(tag):
            return psum[:, plan[index[tag]][0], :]

        def wait_bank(pe, tag):
            n = index[tag]
            before = [m for m in range(n) if plan[m][0] == plan[n][0]]
            if before:
                by = plan[before[-1]][1]
                pe.wait_ge(evac_sem[by], sum(b == by for _, b in plan[:before[-1] + 1]))

        for c in range(KC):
            ring(f"hT{c}", "AV"[c % 2])
        ring("hTm", "V")
        for c in range(CH):
            ring(f"zp{c}", "V")
        for c in range(CH):
            ring(f"u{c}", "A")
        ring("um", "V")
        for c in range(CH):
            ring(f"k{c}", "A")
        ring("km", "V")
        ring("f", "V")
        ring("fm", "V")
        for c in range(CH):
            ring(f"q{c}", "A")
        for t in range(NT):
            ring(f"v{t}", "A")
        ring("vm", "V")
        for c in range(CH):
            ring(f"pm{c}", "V")
        for c in range(CH):
            ring(f"za{c}", "V")
        before_attention = len(plan)
        GATES = [(s, c) for s in range(2) for c in range(KC)]
        for s, c in GATES:
            group(f"g{s}{c}", 7, "A")
        for c in range(KC):
            ring(f"up0{c}", "V")
            ring(f"up1{c}", "V")
        for t in range(NT):
            for e in range(2):
                ring(f"y{t}{e}", "V")
            for j in range(2):
                if t:
                    ring(f"x2T{t - 1}{j}", "V")
        for j in range(2):
            ring(f"x2T{NT - 1}{j}", "V")
        for c in range(CH):
            ring(f"sq{c}", "A")
        for c in range(CH):
            ring(f"sk{c}", "A")
        for t in range(NT):
            ring(f"sv{t}", "A")
        for t in range(NT):
            ring(f"cq{t}", "A")
            ring(f"ckv{t}", "A")
        ring("cqT0", "V")
        ring("ckvT0", "V")
        for t in range(NT):
            for j in range(2):
                ring(f"uq{t}{j}", "A")
            for j in range(2):
                ring(f"ukv{t}{j}", "A")
            if t + 1 < NT:
                ring(f"cqT{t + 1}", "V")
                ring(f"ckvT{t + 1}", "V")
            for j in range(2):
                for g in range(2):
                    ring(f"qkT{t}{j}{g}", "A")
        all_dense_a = sum(b == "A" for _, b in plan)
        all_dense_v = sum(b == "V" for _, b in plan)

        w_in = a["w_in"][0]
        w_in2 = a["w_in_2"][0]

        def chunks(w):
            return w.rearrange("(c p) n -> p c n", p=P)

        U, Z, Q, K, V, ZA, F, G0, G1 = 0, 512, 1024, 1536, 2048, 2560, 3072, 3080, 4104
        units = [("zp", chunks(w_in[:, Z:Z + 512])), ("u", chunks(w_in[:, U:U + 512])),
                 ("k", chunks(w_in[:, K:K + 512])), ("q", chunks(w_in[:, Q:Q + 512])),
                 ("v", chunks(w_in[:, V:V + 512])), ("za", chunks(w_in[:, ZA:ZA + 512]))]
        last_use = {"zp": "zp3", "u": "um", "k": "km", "q": "q3", "v": "vm", "za": "za3"}
        for s, g0 in enumerate((G0, G1)):
            for j in range(2):
                units.append((f"g{s}{j}", chunks(w_in[:, g0 + 512 * j:g0 + 512 * j + 512])))
                last_use[f"g{s}{j}"] = f"g{s}{4 * j + 3}"
        units += [("wup0", chunks(a["w_up_pool"][0])), ("wup1", chunks(a["w_up_attn"][0]))]
        last_use["wup0"] = last_use["wup1"] = "up17"
        for j in range(2):
            units.append((f"wout{j}", chunks(a["w_out"][0][512 * j:512 * j + 512])))
            last_use[f"wout{j}"] = "y31"
        units += [("sq", chunks(w_in2[:, 0:512])), ("sk", chunks(w_in2[:, 512:1024])),
                  ("sv", chunks(w_in2[:, 1024:1536])), ("cq", chunks(w_in2[:, 1536:1920])),
                  ("ckv", chunks(w_in2[:, 1920:2208])), ("uq", chunks(a["w_uq_2"][0])),
                  ("ukv", chunks(a["w_ukv_2"][0]))]
        last_use |= {"sq": "sq3", "sk": "sk3", "sv": "sv3", "cq": "cq3", "ckv": "ckv3",
                     "uq": "uq31", "ukv": "ukv31"}
        for j in range(2):
            units.append((f"wo{j}", chunks(a["w_o_2"][0][512 * j:512 * j + 512])))
        units.append(("subk", a["peer_sub_keys_2"][0].rearrange("c h n d -> n (c h) d")))
        for j in range(4):
            units.append((f"pq{j}", chunks(a["peer_w_q_2"][0][:, 512 * j:512 * j + 512])))
        unit = {name: n for n, (name, _) in enumerate(units)}

        def weights(name):
            n = unit[name]
            _, src = units[n]
            c, w = src.shape[1], src.shape[2]
            return wring[:, n % SLOTS, 0:c * w].rearrange("p (c w) -> p c w", c=c)

        def wait_weights(pe, name):
            n = unit[name]
            pe.wait_ge(w_landed[n % SLOTS], 16 * (n // SLOTS + 1))

        ATT = [(i, h) for i in range(NT) for h in range(H)]
        N1 = N2 = len(ATT)

        WO_AT = (2, 3, 4, 5)

        def wo_bank(i, g):
            return (7, 4, 5, 6)[g] if i == NT - 1 else 7

        def prep_ps(n):
            return psum[:, (0, 2, 1, 3)[n % 4], :]

        def meta_ps(n, i):
            if i < NT - 1:
                return psum[0:META, 4 + n % 2, 3 * P:4 * P]
            return psum[0:META, 2 * (n % 2) + 1, P:2 * P]

        CHUNKS = NT * H
        GATHERS = 2 * CHUNKS * TOPK

        def gather_of(g):
            if g < TOPK:
                return "u", 0, g
            k, j = divmod(g - TOPK, 2 * TOPK)
            if k < CHUNKS - 1 and j < TOPK:
                k, kind = k + 1, "u"
            else:
                kind = "v"
            return kind, k // H, (k % H) * TOPK + j % TOPK

        def u_gather(t, s):
            k = H * t + s // TOPK
            return (TOPK + 2 * TOPK * (k - 1) if k else 0) + s % TOPK

        def v_gather(t, s):
            k = H * t + s // TOPK
            return TOPK + 2 * TOPK * k + (TOPK if k < CHUNKS - 1 else 0) + s % TOPK

        PREP = [("xT", 0), ("xT", 1)] + [(kind, j) for j in range(4) for kind in ("q", "s")]
        SUBK_GROUPS = 4
        PREP_AT = [(), (), (0, 1), (2, 3), (4, 5), (6, 7), (8, 9), ()]
        NORM_AT = 1
        AHEAD = 2
        SMALL = 16 * 14

        block = ctx.enter_context(nc.Block())

        @block.sync
        def _(sp):
            for n, (name, src) in enumerate(units):
                if n >= SLOTS:
                    old = units[n - SLOTS][0]
                    if old in last_use:
                        sp.wait_ge(dense_done, index[last_use[old]] + 1)
                    else:
                        sp.wait_ge(wo_done, 4 * NT)
                if n == 1:
                    sp.wait_ge(x_in, 16 * (NT + 1))
                sp.dma_start(weights(name), src).then_inc(w_landed[n % SLOTS], 16)
            for t in range(NT):
                sp.wait_ge(acc_read, t + 1)
                sp.dma_start(out[0, t * P:(t + 1) * P, :], ostage[:]).then_inc(out_sent, 16)
            sp.wait_ge(out_sent, 16 * NT)

        @block.gpsimd
        def _(gp):
            count = [0]

            def link(ins):
                count[0] += 1
                ins.then_inc(pool_chain, 1)
                gp.wait_ge(pool_chain, count[0])

            nc.gpsimd.memset(ones[:], 1.0)
            nc.gpsimd.memset(neg_half[:], -0.5)
            nc.gpsimd.memset(sel8[:], 0.0)
            nc.gpsimd.memset(masks[:], 0.0)
            for j in range(ROPE // 2):
                nc.gpsimd.memset(freq[:, j:j + 1], float(INV_FREQ[j]))
            nc.gpsimd.memset(identb[:], 0.0)
            link(nc.gpsimd.memset(ident[:], 0.0))
            for m in (ident, identb):
                nc.gpsimd.affine_select(out=m[:], in_=m[:], compare_op=ALU.not_equal, fill=1.0, base=0,
                                        pattern=[[-1, P]], channel_multiplier=1)
            nc.gpsimd.affine_select(out=sel8[:], in_=sel8[:], compare_op=ALU.not_equal, fill=1.0, base=0,
                                    pattern=[[-1, H], [0, P]], channel_multiplier=1)
            for m in range(2):
                nc.gpsimd.affine_select(out=masks[:, m, :], in_=masks[:, m, :], compare_op=ALU.is_ge, fill=NEG,
                                        base=-m, pattern=[[-1, P]], channel_multiplier=1)
            nc.gpsimd.iota(iota[:], [[1, TOPK]], base=0, channel_multiplier=0,
                           allow_small_or_imprecise_dtypes=True)
            link(nc.gpsimd.memset(masks[0:64, 2, 64:P], NEG))
            gp.sem_inc(consts, 1)

            def rstd(ss_ap, out_ap, wait_s, wait_n, scale=1.0):
                gp.wait_ge(wait_s, wait_n)
                link(nc.gpsimd.tensor_scalar(ss_ap, ss_ap, scale, EPS, ALU.mult, ALU.add))
                rows, n = ss_ap.shape
                return nc.gpsimd.tensor_tensor(out_ap, ss_ap, neg_half[0:rows, 0:n], ALU.pow)

            rstd(stat[:, 0:4], stat[:, 8:12], ss_done, 5).then_inc(rstd_done, 1)
            rstd(stat[0:META, 4:5], stat[0:META, 12:13], ss_done, 5).then_inc(rstd_done, 1)
            for t in range(NT):
                rstd(stat[:, 16 + t:17 + t], stat[:, 20 + t:21 + t], ms_done, 2 * t + 1).then_inc(rstd_done, 1)
                rstd(stat[:, 24 + t:25 + t], stat[:, 28 + t:29 + t], ms_done, 2 * t + 2).then_inc(rstd_done, 1)
            for t in range(NT):
                rstd(stat[:, 32 + t:33 + t], stat[:, 40 + t:41 + t], ms_done, 2 * NT + 2 * t + 2, 1.0 / CQ)\
                    .then_inc(rstd_done, 1)
                rstd(stat[:, 36 + t:37 + t], stat[:, 44 + t:45 + t], ms_done, 2 * NT + 2 * t + 2, 1.0 / CKV)\
                    .then_inc(rstd_done, 1)
            for t in range(NT):
                rstd(stat[:, 48:64], stat[:, 64:80], row_sq, 2 * t + 2, 1.0 / QK).then_inc(rstd_done, 1)
            for t in range(NT):
                if t == NT - 1:
                    rstd(stat[:, 84:85], stat[:, 88:89], p_ss, 1).then_inc(p_rstd, 1)
                rstd(stat[:, 80:82], stat[:, 82:84], oms_done, t + 1, 1.0 / T).then_inc(orstd_done, 1)

            gp.wait_ge(oss_done, NT * CH)
            for g in range(GATHERS):
                kind, t, s = gather_of(g)
                if kind == "u" and s % TOPK == 0:
                    gp.wait_ge(idx_ready, H * t + s // TOPK + 1)
                if g == TOPK:
                    rstd(stat[:, 85:88], stat[:, 89:92], p_ss, NT).then_inc(p_rstd, 1)
                if g == AFTER:
                    gp.wait_ge(wo_done, 4 * NT)
                if g >= NB:
                    was, wt, ws = gather_of(g - NB)
                    gp.wait_ge(u_used if was == "u" else v_used, H * TOPK * wt + ws + 1)
                table = a["peer_u_2" if kind == "u" else "peer_v_2"][0]
                nc.gpsimd.indirect_dma_start(gathered[g % NB][:], None, table,
                                             bass.IndirectOffsetOnAxis(ap=idx[:, t % 2, s:s + 1], axis=0))\
                    .then_inc(landed[g % NB], 16)

        @block.scalar
        def _(act):
            done = [0]
            count = [0]

            def link(ins):
                count[0] += 1
                ins.then_inc(act_chain, 1)
                act.wait_ge(act_chain, count[0])

            def freed(ins, tag):
                done[0] += 1
                assert evac_count(tag) == (act_evac, done[0]), tag
                ins.then_inc(act_evac, 1)

            for t in range(NT):
                act.dma_start(xs[:, t, :], a["x"][0, t * P:(t + 1) * P, :]).then_inc(x_in, 16)
            act.dma_start(xmeta[0:META, :], a["meta_tokens"]).then_inc(x_in, 16)

            def column(at, n, src):
                act.dma_start(gains[:, at:at + n], src.rearrange("(c p) -> p c", p=P),
                              allow_slow_non_contiguous=True).then_inc(small_in, 16)

            column(GN, 8, a["norm_g"][0])
            column(GP, 4, a["pool_scale"][0])
            column(GA2, 8, a["attn_norm_2"][0])
            column(GC, 3, a["cq_norm_2"][0])
            column(GKV, 2, a["ckv_norm_2"][0])
            column(GSB, 4, a["sb_out_norm_2"][0])
            column(GML, 4, a["mla_out_norm_2"][0])
            act.dma_start(gains[0:H, 40:41], a["b_forget"].rearrange("a h -> h a"),
                          allow_slow_non_contiguous=True).then_inc(small_in, 16)
            act.dma_start(f_w[:], chunks(w_in[:, F:F + H]), allow_slow_non_contiguous=True).then_inc(small_in, 16)
            act.dma_start(poolw[:], a["pool_w"][0].rearrange("g c d -> c g d")).then_inc(small_in, 16)
            act.dma_start(posi[:], a["positions_2"].rearrange("a (t p) -> p (a t)", p=P),
                          allow_slow_non_contiguous=True).then_inc(small_in, 16)
            act.dma_start(gain_row[:], a["final_norm_g"].partition_broadcast(P)).then_inc(small_in, 16)
            act.dma_start(qk_gain[:, 0, :], a["q_norm_2"][0].partition_broadcast(P)).then_inc(small_in, 16)
            act.dma_start(qk_gain[:, 1, :], a["k_norm_2"][0].partition_broadcast(P)).then_inc(small_in, 16)

            act.wait_ge(x_in, 16 * (NT + 1))
            for t in range(NT):
                if t:
                    act.wait_ge(ss_done, t)
                nc.scalar.activation(junk[:], xs[:, t, :], ACT.Square, scale=1 / 32,
                                     accum_out=stat[:, t:t + 1]).then_inc(ss_done, 1)
            act.wait_ge(ss_done, NT)
            nc.scalar.activation(junk[0:META, :], xmeta[0:META, :], ACT.Square, scale=1 / 32,
                                 accum_out=stat[0:META, 4:5]).then_inc(ss_done, 1)
            act.wait_ge(small_in, SMALL)
            for c in range(0, KC, 2):
                wait_group(act, f"hT{c}")
                freed(nc.scalar.activation(hT[:, c, META:L], bank(f"hT{c}"), ACT.Copy,
                                           scale=gains[:, GN + c:GN + c + 1]), f"hT{c}")
            for c in range(CH):
                wait_group(act, f"zp{c}")
                nc.scalar.activation(zp[:, c, :], bank(f"zp{c}"), ACT.Tanh, scale=0.5).then_inc(tanh_done, 1)
            act.wait_ge(xn_done, NT + 1)
            wait_group(act, "hTm")
            for c in range(CH):
                wait_group(act, f"u{c}")
                freed(nc.scalar.copy(uT[:, c, META:L], bank(f"u{c}")), f"u{c}")
            for c in range(CH):
                wait_group(act, f"k{c}")
                freed(nc.scalar.copy(kT[:, c, META:L], bank(f"k{c}")), f"k{c}")
            act.wait_ge(decay_x, 1)
            link(nc.scalar.activation(lf[0:H, 1, :], lf[0:H, 0, :], ACT.Abs))
            link(nc.scalar.activation(lf[0:H, 1, :], lf[0:H, 1, :], ACT.Exp, scale=-1.0))
            nc.scalar.activation(lf[0:H, 1, :], lf[0:H, 1, :], ACT.Ln, bias=1.0).then_inc(decay_ln, 1)
            for c in range(CH):
                wait_group(act, f"q{c}")
                freed(nc.scalar.activation(qT[:, c, :], bank(f"q{c}"), ACT.Copy, scale=HD ** -0.5), f"q{c}")
            for t in range(NT):
                wait_group(act, f"v{t}")
                freed(nc.scalar.copy(vtok[:, t, :], bank(f"v{t}")), f"v{t}")
            for c in range(CH):
                wait_group(act, f"za{c}")
                nc.scalar.activation(za[:, c, :], bank(f"za{c}"), ACT.Tanh, scale=0.5).then_inc(tanh_done, 1)

            def copy_pT(n, i):
                act.wait_ge(pT_done, n + 1)
                if n >= 2:
                    act.wait_ge(pv_done, n - 1)
                w = (i + 1) * P
                nc.scalar.copy(PT[:, n % 2, 0:i + 1, :],
                               psum[:, 4 + n % 2, 0:w].rearrange("p (a b) -> p a b", b=P))
                nc.scalar.copy(PT[0:META, n % 2, 4, :], meta_ps(n, i)).then_inc(pT_copied, 1)

            act.wait_ge(pooled, 1 + CH)
            for n, (i, h) in enumerate(ATT):
                w = (i + 1) * P + META
                act.wait_ge(max_done, n + 1)
                if n >= 2:
                    act.wait_ge(pT_done, n - 1)
                s_ps = psum[:, 2 * (n % 2):2 * (n % 2) + 2, :].rearrange("p a b -> p (a b)")
                nc.scalar.activation(Pb[:, n % 2, 0:w], s_ps[:, 0:w], ACT.Exp, bias=stat[:, 96 + n % 4:97 + n % 4],
                                     accum_out=stat[:, 100 + n % 4:101 + n % 4]).then_inc(exp_done, 1)
                if n:
                    copy_pT(n - 1, ATT[n - 1][0])
                if n % 2 == 1:
                    s, c = GATES[n // 2]
                    wait_group(act, f"g{s}{c}")
                    freed(nc.scalar.activation(gate[:, s, c, :], bank(f"g{s}{c}"), ACT.Tanh, scale=0.5), f"g{s}{c}")
            copy_pT(N1 - 1, NT - 1)
            for t in range(NT):
                act.dma_start(x1[:, t, :], a["x"][0, t * P:(t + 1) * P, :]).then_inc(xres_in, 16)

            nc.scalar.preload_act_table_set("natural_log_exp_and_others")
            for t in range(NT):
                act.wait_ge(x1_done, 2 * t + 1)
                nc.scalar.activation(junk[:], x1[:, t, :], ACT.Square, scale=1 / 32,
                                     accum_out=stat[:, 16 + t:17 + t]).then_inc(ms_done, 1)
                act.wait_ge(x1_done, 2 * t + 2)
                act.wait_ge(ms_done, 2 * t + 1)
                nc.scalar.activation(junk[:], x1[:, t, :], ACT.Square, scale=1 / 32,
                                     accum_out=stat[:, 24 + t:25 + t]).then_inc(ms_done, 1)
                act.wait_ge(ms_done, 2 * t + 2)
            act.dma_start(gain_row[:], a["ffn_norm_2"][0].partition_broadcast(P)).then_inc(grow_in, 16)

            act.wait_ge(rope_arg, 1)
            nc.scalar.activation(trig[:], trig[:], ACT.Sin).then_inc(trig_done, 1)
            nc.scalar.preload_act_table_set("natural_log_exp_and_others")
            for c in range(CH):
                wait_group(act, f"sq{c}")
                freed(nc.scalar.activation(sq[:, c, :], bank(f"sq{c}"), ACT.Copy, scale=HD ** -0.5), f"sq{c}")
            for c in range(CH):
                wait_group(act, f"sk{c}")
                freed(nc.scalar.copy(sk[:, c, :], bank(f"sk{c}")), f"sk{c}")
            for t in range(NT):
                wait_group(act, f"sv{t}")
                freed(nc.scalar.copy(sv[:, t, :], bank(f"sv{t}")), f"sv{t}")
            wait_group(act, "x2T31")
            for t in range(NT):
                wait_group(act, f"cq{t}")
                nc.scalar.copy(cqt[:, t, 0:CQ], bank(f"cq{t}")[:, 0:CQ])
                nc.scalar.activation(rsq_junk[:, 0:CQ], bank(f"cq{t}")[:, 0:CQ], ACT.Square,
                                     accum_out=stat[:, 32 + t:33 + t]).then_inc(ms_done, 1)
                act.wait_ge(ms_done, 2 * NT + 2 * t + 1)
                act.sem_inc(act_evac, 1)
                wait_group(act, f"ckv{t}")
                nc.scalar.copy(cqt[:, t, CQ:672], bank(f"ckv{t}")[:, 0:CKV + ROPE])
                nc.scalar.activation(rsq_junk[:, 0:CKV], bank(f"ckv{t}")[:, 0:CKV], ACT.Square,
                                     accum_out=stat[:, 36 + t:37 + t]).then_inc(ms_done, 1)
                act.wait_ge(ms_done, 2 * NT + 2 * t + 2)
                act.sem_inc(act_evac, 1)
                done[0] += 2
            wait_group(act, "ckv3")
            for t in range(NT):
                for j in range(2):
                    wait_group(act, f"uq{t}{j}")
                    if t and not j:
                        wait_group(act, f"qkT{t - 1}11")
                        act.wait_ge(rope_done, 2 * t)
                    freed(nc.scalar.copy(rows[:, 0, 4 * j:4 * j + 4, :],
                                         bank(f"uq{t}{j}")[:, 0:4 * QK].rearrange("p (h d) -> p h d", h=4)),
                          f"uq{t}{j}")
                for j in range(2):
                    wait_group(act, f"ukv{t}{j}")
                    kv = bank(f"ukv{t}{j}").rearrange("p (h d) -> p h d", h=4)
                    nc.scalar.copy(rows[:, 1, 4 * j:4 * j + 4, 0:HD], kv[:, :, 0:HD])
                    freed(nc.scalar.copy(mv[:, t, :].rearrange("p (h d) -> p h d", h=H)[:, 4 * j:4 * j + 4, :],
                                         kv[:, :, HD:P]), f"ukv{t}{j}")
                link(nc.scalar.copy(rows[:, 1, :, HD:QK],
                                    cqt[:, t, CQ + CKV:672].unsqueeze(1).to_broadcast([P, H, ROPE])))
                for j in range(2):
                    nc.scalar.activation(rsq[:, j], rows[:, j], ACT.Square).then_inc(rows_squared, 1)
                for j in range(2):
                    for g in range(2):
                        wait_group(act, f"qkT{t}{j}{g}")
                        dst = (mq, mk)[j]
                        freed(nc.scalar.copy(dst[0:QK, 4 * g:4 * g + 4, t * P:(t + 1) * P],
                                             bank(f"qkT{t}{j}{g}")[0:QK, :].rearrange("p (h t) -> p h t", h=4)),
                              f"qkT{t}{j}{g}")

            def copy_pT2(p, kind):
                i = ATT[p][0]
                act.wait_ge(pT2_done[kind], p + 1)
                if p:
                    act.wait_ge(pv2_done, p)
                nc.scalar.copy(PT2[:, kind, 0:i + 1, :],
                               psum[:, 4 + kind, 0:(i + 1) * P].rearrange("p (a b) -> p a b", b=P))\
                    .then_inc(pT2_copied[kind], 1)

            def softplus(p):
                w = (ATT[p][0] + 1) * P
                buf = soft_z[:, p % 2, 0:w]
                act.wait_ge(s2_done[0], p + 1)
                if p >= 2:
                    act.wait_ge(zr_done, p - 1)
                nc.scalar.activation(buf, psum[:, p % 2, 0:w], ACT.Abs).then_inc(z_abs, 1)
                act.wait_ge(z_abs, p + 1)
                link(nc.scalar.activation(buf, buf, ACT.Exp, scale=-1.0))
                nc.scalar.activation(buf, buf, ACT.Ln, bias=1.0).then_inc(sp_done, 1)

            def squares(q):
                act.wait_ge(pv2_done, 2 * q + 2)
                if q >= 2:
                    act.wait_ge(oss_done, q - 1)
                nc.scalar.activation(osq[:, q % 2], psum[:, 6, 0:2 * P].rearrange("p (a b) -> p a b", a=2),
                                     ACT.Square).then_inc(osq_done, 1)

            softplus(0)
            for p, (i, h) in enumerate(ATT):
                w = (i + 1) * P
                if p + 1 < N2:
                    softplus(p + 1)
                else:
                    act.wait_ge(s2_done[0], N2)
                    act.wait_ge(s2_done[1], N2)
                    act.wait_ge(x2_added, 4)
                    nc.scalar.activation(pq[:, 0:KC, :].rearrange("p a b -> p (a b)"), x1[:, 0, :], ACT.Square,
                                         scale=1 / 32, accum_out=stat[:, 84:85]).then_inc(p_ss, 1)
                if p:
                    copy_pT2(p - 1, 0)
                    copy_pT2(p - 1, 1)
                act.wait_ge(ml_max, p + 1)
                if p:
                    act.wait_ge(pT2_done[1], p)
                nc.scalar.activation(Pb2[:, 1, 0:w], psum[:, 2 + p % 2, 0:w], ACT.Exp,
                                     bias=stat[:, 96 + p % 4:97 + p % 4], scale=QK ** -0.5,
                                     accum_out=stat[:, 100 + p % 4:101 + p % 4]).then_inc(exp2_done[1], 1)
                act.wait_ge(zr_done, p + 1)
                nc.scalar.activation(Pb2[:, 0, 0:w], Pb2[:, 0, 0:w], ACT.Exp).then_inc(exp2_done[0], 1)
                if p % 2 == 0 and p:
                    squares(p // 2 - 1)
            def evac_prep(t, n):
                kind, j = PREP[n]
                act.wait_ge(prep_mm, SUBK_GROUPS + len(PREP) * t + n + 1)
                src = prep_ps(SUBK_GROUPS + len(PREP) * t + n).rearrange("p (a b) -> p a b", b=P)
                dst = {"xT": xnT, "q": pq, "s": sc}[kind][:, 4 * j:4 * j + 4, :]
                if kind == "s" and t:
                    act.wait_ge(top_done, H * (t - 1) + 2 * j + 2)
                nc.scalar.copy(dst, src).then_inc(prep_evac, 1)

            def evac_subk(j):
                act.wait_ge(prep_mm, j + 1)
                nc.scalar.copy(skT[:, 4 * j:4 * j + 4, :], prep_ps(j).rearrange("p (a b) -> p a b", b=P))\
                    .then_inc(prep_evac, 1)

            copy_pT2(N2 - 1, 0)
            copy_pT2(N2 - 1, 1)
            for j in range(SUBK_GROUPS):
                evac_subk(j)
            squares(N2 // 2 - 1)

            act.wait_ge(p_ss, 1)
            for n in range(len(PREP)):
                evac_prep(0, n)

            def exp_soft(k):
                t, c = divmod(k, H)
                cols = slice(c * TOPK, (c + 1) * TOPK)
                act.wait_ge(soft_in, k + 1)
                nc.scalar.activation(soft[:, t % 2, cols], soft[:, t % 2, cols], ACT.Exp,
                                     accum_out=stat[:, 110 + k % 4:111 + k % 4]).then_inc(soft_exp, 1)

            for k in range(AHEAD):
                exp_soft(k)
            act.wait_ge(x2_added, 4 * NT)
            for t in range(1, NT):
                act.wait_ge(p_ss, t)
                nc.scalar.activation(ostage[:], x1[:, t, :], ACT.Square, scale=1 / 32,
                                     accum_out=stat[:, 84 + t:85 + t]).then_inc(p_ss, 1)

            def gelu_part(t, c):
                act.wait_ge(u_used, (H * t + c + 1) * TOPK)
                nc.scalar.activation(gel[:, c * TOPK:(c + 1) * TOPK], pre[:, c * TOPK:(c + 1) * TOPK], ACT.Gelu)\
                    .then_inc(gelu_done, 1)

            def diagonals(t, c):
                act.wait_ge(coef_done, H * t + c + 1)
                for s in range(c * TOPK, (c + 1) * TOPK):
                    n = H * TOPK * t + s
                    if n >= 4:
                        act.wait_ge(v_used, n - 3)
                    nc.scalar.activation(diag[:, n % 4, :], ident[:], ACT.Copy, scale=coef[:, s:s + 1])\
                        .then_inc(diag_done, 1)

            for t in range(NT):
                for c in range(H):
                    gelu_part(t, c)
                    if H * t + c + AHEAD < CHUNKS:
                        exp_soft(H * t + c + AHEAD)
                    diagonals(t, c)
                    if t + 1 < NT:
                        for n in PREP_AT[c]:
                            evac_prep(t + 1, n)

        @block.vector
        def _(dve):
            done = [0]
            count = [0]

            def link(ins):
                count[0] += 1
                ins.then_inc(dve_chain, 1)
                dve.wait_ge(dve_chain, count[0])

            def freed(ins, tag):
                done[0] += 1
                assert evac_count(tag) == (dve_evac, done[0]), tag
                ins.then_inc(dve_evac, 1)

            dve.wait_ge(x_in, 16 * (NT + 1))
            dve.wait_ge(rstd_done, 1)
            for t in range(NT):
                nc.vector.tensor_scalar(xs[:, t, :], xs[:, t, :], stat[:, 8 + t:9 + t], None, ALU.mult)\
                    .then_inc(xn_done, 1)
            dve.wait_ge(rstd_done, 2)
            nc.vector.tensor_scalar(xmeta[0:META, :], xmeta[0:META, :], stat[0:META, 12:13], None, ALU.mult)\
                .then_inc(xn_done, 1)
            dve.wait_ge(small_in, SMALL)
            for c in range(1, KC, 2):
                wait_group(dve, f"hT{c}")
                freed(nc.vector.tensor_scalar(hT[:, c, META:L], bank(f"hT{c}"), gains[:, GN + c:GN + c + 1], None,
                                              ALU.mult), f"hT{c}")
            wait_group(dve, "hTm")
            freed(nc.vector.tensor_tensor(hT[:, :, 0:META], bank("hTm")[:, 0:P].rearrange("p (c m) -> p c m", c=KC),
                                          gains[:, GN:GN + KC].unsqueeze(2).to_broadcast([P, KC, META]), ALU.mult),
                  "hTm")
            for c in range(CH):
                dve.wait_ge(tanh_done, c + 1)
                freed(nc.vector.scalar_tensor_tensor(zp[:, c, :], zp[:, c, :], 1.0, bank(f"zp{c}"), ALU.add, ALU.mult),
                      f"zp{c}")
            wait_group(dve, "um")
            freed(nc.vector.tensor_copy(uT[:, :, 0:META], bank("um")[:, 0:CH * META]
                                        .rearrange("p (c m) -> p c m", c=CH)), "um")
            wait_group(dve, "km")
            freed(nc.vector.tensor_copy(kT[:, :, 0:META], bank("km")[:, 0:CH * META]
                                        .rearrange("p (c m) -> p c m", c=CH)), "km")
            wait_group(dve, "f")
            freed(nc.vector.tensor_scalar(lf[0:H, 0, META:L], bank("f")[0:H, :], gains[0:H, 40:41], None, ALU.add), "f")
            wait_group(dve, "fm")
            freed(nc.vector.tensor_scalar(lf[0:H, 0, 0:META], bank("fm")[0:H, 0:META], gains[0:H, 40:41], None,
                                          ALU.add), "fm")
            wait_evac(dve, "fm")
            dve.sem_inc(decay_x, 1)
            wait_evac(dve, "u3")
            wait_evac(dve, "um")
            for c in range(CH):
                src, left = uT[:, c, :], 0
                for s in range(c + 1):
                    step = 1 << s
                    dst = win[:, s % 2, :]
                    left += step
                    link(nc.vector.tensor_tensor(dst[:, left:L], src[:, left:L], src[:, left - step:L - step], ALU.add))
                    src = dst
                link(nc.vector.scalar_tensor_tensor(uT[:, c, META:L], src[:, META:L], 1.0 / (2 << c), uT[:, c, META:L],
                                                    ALU.mult, ALU.subtract))
                dve.sem_inc(pooled, 1)
            dve.wait_ge(decay_ln, 1)
            link(nc.vector.tensor_scalar(lf[0:H, 0, :], lf[0:H, 0, :], 0.0, None, ALU.min))
            nc.vector.tensor_tensor_scan(negc[:], lf[0:H, 1, :], lf[0:H, 0, :], 0.0, ALU.add, ALU.subtract)\
                .then_inc(decay_done, 1)
            link(nc.vector.tensor_scalar(gains[:, GP:GP + CH], gains[:, GP:GP + CH], 0.5, None, ALU.mult))
            wait_group(dve, "vm")
            freed(nc.vector.tensor_copy(vmeta[0:META, :], bank("vm")[0:META, :]), "vm")
            for c in range(CH):
                wait_group(dve, f"pm{c}")
                freed(nc.vector.scalar_tensor_tensor(zp[:, c, :], bank(f"pm{c}"), gains[:, GP + c:GP + c + 1],
                                                     zp[:, c, :], ALU.mult, ALU.mult), f"pm{c}")
            for c in range(CH):
                dve.wait_ge(tanh_done, CH + c + 1)
                freed(nc.vector.scalar_tensor_tensor(za[:, c, :], za[:, c, :], 1.0, bank(f"za{c}"), ALU.add, ALU.mult),
                      f"za{c}")
            wait_evac(dve, "za3")
            dve.sem_inc(pooled, 1)

            def normalise(n, i, buf, w, half, base):
                dve.wait_ge(exp_done, base + n + 1)
                link(nc.vector.reciprocal(stat[:, 104 + n % 4:105 + n % 4], stat[:, 100 + n % 4:101 + n % 4]))
                nc.vector.tensor_scalar(buf[:, n % 2, 0:w], buf[:, n % 2, 0:w], stat[:, 104 + n % 4:105 + n % 4],
                                        half, ALU.mult, ALU.mult).then_inc(norm_done, 1)

            def gated(n):
                i, h = ATT[n]
                dve.wait_ge(pv_done, n + 1)
                cols = za[:, h // 2, i * P:(i + 1) * P]
                nc.vector.tensor_tensor(cols, psum[:, 6, 0:P], cols, ALU.mult).then_inc(y_done, 1)

            for n, (i, h) in enumerate(ATT):
                w = (i + 1) * P + META
                dve.wait_ge(s_done, n + 1)
                s_ps = psum[:, 2 * (n % 2):2 * (n % 2) + 2, :].rearrange("p a b -> p (a b)")
                if n >= 4:
                    dve.wait_ge(norm_done, n - 3)
                nc.vector.tensor_reduce(stat[:, 96 + n % 4:97 + n % 4], s_ps[:, 0:w], AX, ALU.max, negate=True)\
                    .then_inc(max_done, 1)
                if n:
                    pi = ATT[n - 1][0]
                    normalise(n - 1, pi, Pb, (pi + 1) * P + META, 0.5, 0)
                if n >= 4 and n % 2 == 0:
                    gated(n - 3)
            normalise(N1 - 1, NT - 1, Pb, L, 0.5, 0)
            gated(N1 - 3)
            gated(N1 - 1)

            for c in range(KC):
                for s in range(2):
                    wait_group(dve, f"up{s}{c}")
                    if s == 0 and c == 0:
                        wait_evac(dve, "g17")
                    freed(nc.vector.scalar_tensor_tensor(gate[:, s, c, :], gate[:, s, c, :], 1.0, bank(f"up{s}{c}"),
                                                         ALU.add, ALU.mult), f"up{s}{c}")
                wait_evac(dve, f"up1{c}")
                nc.vector.tensor_tensor(gate[:, 0, c, :], gate[:, 0, c, :], gate[:, 1, c, :], ALU.add)\
                    .then_inc(merged_done, 1)
            dve.wait_ge(xres_in, 16 * NT)

            def x2T_evac(t):
                for j in range(2):
                    wait_group(dve, f"x2T{t}{j}")
                    freed(nc.vector.tensor_tensor(x2T[:, 4 * j:4 * j + 4, t * P:(t + 1) * P],
                                                  bank(f"x2T{t}{j}").rearrange("p (c t) -> p c t", c=4),
                                                  gains[:, GA2 + 4 * j:GA2 + 4 * j + 4].unsqueeze(2)
                                                  .to_broadcast([P, 4, P]), ALU.mult), f"x2T{t}{j}")

            for t in range(NT):
                for e in range(2):
                    wait_group(dve, f"y{t}{e}")
                    freed(nc.vector.scalar_tensor_tensor(x1[:, t, 512 * e:512 * e + 512], bank(f"y{t}{e}"), 0.5,
                                                         x1[:, t, 512 * e:512 * e + 512], ALU.mult, ALU.add),
                          f"y{t}{e}")
                wait_evac(dve, f"y{t}1")
                dve.sem_inc(x1_done, 1)
                dve.wait_ge(rstd_done, 2 + 2 * t + 1)
                nc.vector.scalar_tensor_tensor(x1[:, t, :], x1[:, t, :], stat[:, 20 + t:21 + t], gain_row[:],
                                               ALU.mult, ALU.mult).then_inc(x1_done, 1)
                dve.wait_ge(x1_done, 2 * t + 2)
                dve.wait_ge(rstd_done, 2 + 2 * t + 2)
                if t >= 2:
                    wait_group(dve, f"x2T{t - 2}1")
                nc.vector.tensor_scalar(xn2[:, t % 2, :], x1[:, t, :], stat[:, 28 + t:29 + t], None, ALU.mult)\
                    .then_inc(xn_done, 1)
                if t:
                    x2T_evac(t - 1)
            x2T_evac(NT - 1)

            dve.wait_ge(consts, 1)
            link(nc.vector.tensor_copy(posf[:], posi[:]))
            for t in range(NT):
                link(nc.vector.tensor_scalar(trig[:, 1, t, :], freq[:], posf[:, t:t + 1], None, ALU.mult))
            turns = 1 / TWO_PI
            ang = trig[:, 1].rearrange("p t r -> p (t r)")
            for q in range(2):
                link(nc.vector.tensor_scalar(angle[:, q, :], ang, turns, 0.25 * (1 - q), ALU.mult, ALU.add))
                link(nc.vector.tensor_scalar(angle[:, q, :], angle[:, q, :], MAGIC, -MAGIC, ALU.add, ALU.add))
            for q in range(2):
                r = trig[:, q].rearrange("p t r -> p (t r)")
                src = ang
                for part in (TP1, TP2, TP3):
                    link(nc.vector.scalar_tensor_tensor(r, angle[:, q, :], -part, src, ALU.mult, ALU.add))
                    src = r
                if q == 0:
                    link(nc.vector.tensor_scalar(r, r, float(np.pi / 2), None, ALU.add))
                link(nc.vector.tensor_scalar(r, r, 3.1415925, -3.1415925, ALU.min, ALU.max))
            dve.sem_inc(rope_arg, 1)

            for t in range(NT):
                dve.wait_ge(rstd_done, 2 + 2 * NT + 2 * t + 2)
                nc.vector.tensor_scalar(cqt[:, t, 0:CQ], cqt[:, t, 0:CQ], stat[:, 40 + t:41 + t], None, ALU.mult)\
                    .then_inc(xn_done, 1)
                nc.vector.tensor_scalar(cqt[:, t, CQ:CQ + CKV], cqt[:, t, CQ:CQ + CKV], stat[:, 44 + t:45 + t], None,
                                        ALU.mult).then_inc(xn_done, 1)
            def latents(t):
                for tag, n, c0, g in ((f"cqT{t}", 3, 0, GC), (f"ckvT{t}", 2, 3, GKV)):
                    wait_group(dve, tag)
                    c0 += 5 * (t % 2)
                    freed(nc.vector.tensor_tensor(latT[:, c0:c0 + n, :],
                                                  bank(tag)[:, 0:n * P].rearrange("p (c t) -> p c t", c=n),
                                                  gains[:, g:g + n].unsqueeze(2).to_broadcast([P, n, P]), ALU.mult),
                          tag)
            latents(0)
            dve.wait_ge(trig_done, 1)
            R2 = ROPE // 2
            for t in range(NT):
                if t + 1 < NT:
                    latents(t + 1)
                dve.wait_ge(rows_squared, 2 * t + 2)
                for j in range(2):
                    nc.vector.tensor_reduce(stat[:, 48 + 8 * j:56 + 8 * j], rsq[:, j], AX, ALU.add).then_inc(row_sq, 1)
                dve.wait_ge(rstd_done, 2 + 4 * NT + t + 1)
                for j in range(2):
                    r = rows[:, j]
                    link(nc.vector.tensor_tensor(r, r, stat[:, 64 + 8 * j:72 + 8 * j].unsqueeze(2)
                                                 .to_broadcast([P, H, QK]), ALU.mult))
                    link(nc.vector.tensor_tensor(r, r, qk_gain[:, j, :].unsqueeze(1).to_broadcast([P, H, QK]),
                                                 ALU.mult))
                    a1, a2 = r[:, :, HD:HD + R2], r[:, :, HD + R2:QK]
                    cos = trig[:, 0, t, :].unsqueeze(1).to_broadcast([P, H, R2])
                    sin = trig[:, 1, t, :].unsqueeze(1).to_broadcast([P, H, R2])
                    tm = [rtmp[:, q, 0:H * R2].rearrange("p (h r) -> p h r", h=H) for q in range(4)]
                    nc.vector.tensor_tensor(tm[0], a1, cos, ALU.mult)
                    nc.vector.tensor_tensor(tm[1], a2, sin, ALU.mult)
                    nc.vector.tensor_tensor(tm[2], a1, sin, ALU.mult)
                    link(nc.vector.tensor_tensor(tm[3], a2, cos, ALU.mult))
                    nc.vector.tensor_tensor(a1, tm[0], tm[1], ALU.subtract)
                    link(nc.vector.tensor_tensor(a2, tm[2], tm[3], ALU.add))
                    dve.sem_inc(rope_done, 1)

            def outputs(q):
                i, h = ATT[2 * q]
                dve.wait_ge(osq_done, q + 1)
                for kind in range(2):
                    c = CH * kind + h // 2
                    nc.vector.tensor_scalar(og[:, c, i * P:(i + 1) * P], psum[:, 6, kind * P:(kind + 1) * P],
                                            gains[:, GSB + c:GSB + c + 1], None, ALU.mult).then_inc(og_done, 1)

            def mean_squares(i):
                dve.wait_ge(oss_done, CH * (i + 1))
                nc.vector.tensor_reduce(stat[:, 80:82], psum[:, 6, 2 * P:2 * P + 2 * CH]
                                        .rearrange("p (a b) -> p a b", a=2), AX, ALU.add).then_inc(oms_done, 1)

            def combine(i, g):
                e, kind = divmod(g, 2)
                dve.wait_ge(orstd_done, i + 1)
                dve.wait_ge(wo_done, 4 * i + g + 1)
                if kind:
                    dve.wait_ge(x2_added, 4 * i + g)
                cols = x1[:, i, 512 * e:512 * e + 512]
                nc.vector.scalar_tensor_tensor(cols, psum[:, wo_bank(i, g), :], stat[:, 82 + kind:83 + kind],
                                               cols, ALU.mult, ALU.add).then_inc(x2_added, 1)

            def latent_max(p):
                w = (ATT[p][0] + 1) * P
                dve.wait_ge(s2_done[1], p + 1)
                link(nc.vector.tensor_reduce(stat[:, 108:109], psum[:, 2 + p % 2, 0:w], AX, ALU.max, negate=True))
                nc.vector.tensor_scalar(stat[:, 96 + p % 4:97 + p % 4], stat[:, 108:109], QK ** -0.5, None,
                                        ALU.mult).then_inc(ml_max, 1)

            latent_max(0)
            for p, (i, h) in enumerate(ATT):
                w = (i + 1) * P
                z = psum[:, p % 2, 0:w]
                suffix = soft_z[:, p % 2]
                dve.wait_ge(z_abs, p + 1)
                if p:
                    dve.wait_ge(zr_done, p)
                link(nc.vector.tensor_scalar(relu_z[:, 0:w], z, 0.0, None, ALU.max))
                dve.wait_ge(sp_done, p + 1)
                link(nc.vector.tensor_tensor_scan(suffix[:, w - 1::-1], suffix[:, w - 1::-1], relu_z[:, w - 1::-1],
                                                  0.0, ALU.add, ALU.add))
                if p:
                    dve.wait_ge(pT2_done[0], p)
                nc.vector.tensor_tensor(Pb2[:, 0, 0:w], z, suffix[:, 0:w], ALU.subtract).then_inc(zr_done, 1)
                if p + 1 < N2:
                    latent_max(p + 1)
                if h == 1 and i:
                    mean_squares(i - 1)
                dve.wait_ge(exp2_done[1], p + 1)
                link(nc.vector.reciprocal(stat[:, 104 + p % 4:105 + p % 4], stat[:, 100 + p % 4:101 + p % 4]))
                nc.vector.tensor_scalar(Pb2[:, 1, 0:w], Pb2[:, 1, 0:w], stat[:, 104 + p % 4:105 + p % 4],
                                        None, ALU.mult).then_inc(ml_norm, 1)
                if h % 2 == 0 and p:
                    outputs(p // 2 - 1)
                if h in WO_AT and i:
                    combine(i - 1, WO_AT.index(h))
            def prep_norm(t):
                dve.wait_ge(p_rstd, 1 if t == 0 else 2)
                if t == 0:
                    dve.wait_ge(s2_done[0], N2)
                    dve.wait_ge(s2_done[1], N2)
                    dve.wait_ge(grow_in, 16)
                if t >= 2:
                    dve.wait_ge(u_used, H * TOPK * (t - 1))
                nc.vector.scalar_tensor_tensor(xn[:, t % 2, :], x1[:, t, :], stat[:, 88 + t:89 + t], gain_row[:],
                                               ALU.mult, ALU.mult).then_inc(p_xn, 1)

            prep_norm(0)
            outputs(N2 // 2 - 1)
            mean_squares(NT - 1)

            def prep_top(k):
                t, h = divmod(k, H)
                group = PREP.index(("s", h // 2))
                dve.wait_ge(prep_evac, SUBK_GROUPS + len(PREP) * t + group + 1)
                scores = [sc[:, 2 * h + half, :] for half in range(2)]
                for half in range(2):
                    last = nc.vector.max(tops[:, half, 0:8], scores[half])
                link(last)
                for half in range(2):
                    nc.vector.max_index(topi[:, half, 0:8], tops[:, half, 0:8], scores[half])
                for half in range(2):
                    last = nc.vector.match_replace(spare2[:, half, :], tops[:, half, 0:8], scores[half], BELOW)
                last.then_inc(top_done, 1)
                dve.wait_ge(top_done, k + 1)
                for half in range(2):
                    last = nc.vector.max(tops[:, half, 8:16], spare2[:, half, :])
                link(last)
                link(nc.vector.tensor_tensor(cand.rearrange("p (a b) -> p a b", a=TOPK),
                                             tops[:, 0, :].unsqueeze(2).to_broadcast([P, TOPK, TOPK]),
                                             tops[:, 1, :].unsqueeze(1).to_broadcast([P, TOPK, TOPK]), ALU.add))
                link(nc.vector.max(best[:, 0:8], cand))
                for half in range(2):
                    nc.vector.max_index(topi[:, half, 8:16], tops[:, half, 8:16], spare2[:, half, :])
                nc.vector.max_index(posn[:, 0:8], best[:, 0:8], cand)
                link(nc.vector.match_replace(cand2, best[:, 0:8], cand, BELOW))
                link(nc.vector.max(best[:, 8:16], cand2))
                nc.vector.tensor_copy(topif[:], topi[:])
                link(nc.vector.max_index(posn[:, 8:16], best[:, 8:16], cand2))
                cols = slice(h * TOPK, (h + 1) * TOPK)
                nc.vector.tensor_tensor(soft[:, t % 2, cols], best[:], best[:, 0:1].to_broadcast([P, TOPK]),
                                        ALU.subtract).then_inc(soft_in, 1)
                nc.vector.tensor_scalar(posab[:, 0, :], posn[:], 4, None, ALU.logical_shift_right)
                link(nc.vector.tensor_scalar(posab[:, 1, :], posn[:], TOPK - 1, None, ALU.bitwise_and))
                link(nc.vector.tensor_copy(posf2[:], posab[:]))
                for half in range(2):
                    last = nc.vector.tensor_tensor(onehot[:, half], posf2[:, half, :].unsqueeze(2)
                                                   .to_broadcast([P, TOPK, TOPK]),
                                                   iota[:].unsqueeze(1).to_broadcast([P, TOPK, TOPK]), ALU.is_equal)
                link(last)
                for half in range(2):
                    last = nc.vector.tensor_tensor(onehot[:, half], onehot[:, half], topif[:, half, :].unsqueeze(1)
                                                   .to_broadcast([P, TOPK, TOPK]), ALU.mult)
                link(last)
                link(nc.vector.tensor_reduce(idxf[:, 0:2, :].rearrange("p a b -> p (a b)"),
                                             onehot.rearrange("p a b c -> p (a b) c"), AX, ALU.add))
                link(nc.vector.scalar_tensor_tensor(idxf[:, 2, :], idxf[:, 0, :], float(NK), idxf[:, 1, :], ALU.mult,
                                                    ALU.add))
                if t >= 2:
                    dve.wait_ge(v_used, H * TOPK * (t - 2) + (h + 1) * TOPK)
                nc.vector.tensor_copy(idx[:, t % 2, cols], idxf[:, 2, :]).then_inc(idx_ready, 1)

            prep_top(0)
            for g in range(4):
                combine(NT - 1, g)
            for k in range(1, AHEAD):
                prep_top(k)

            def dots(t, c):
                for s in range(c * TOPK, (c + 1) * TOPK):
                    g = u_gather(t, s)
                    if s % TOPK == 4 and (t or c):
                        weigh(*divmod(H * t + c - 1, H))
                    dve.wait_ge(landed[g % NB], 16 * (g // NB + 1))
                    if t and s % TOPK == 0:
                        dve.wait_ge(gelu_done, H * (t - 1) + c + 1)
                    nc.vector.tensor_tensor_reduce(out=gathered[g % NB][:], in0=gathered[g % NB][:],
                                                   in1=xn[:, t % 2, :], scale=1.0, scalar=0.0, op0=ALU.mult,
                                                   op1=ALU.add, accum_out=pre[:, s:s + 1]).then_inc(u_used, 1)

            def weigh(t, c):
                k = H * t + c
                cols = slice(c * TOPK, (c + 1) * TOPK)
                dve.wait_ge(soft_exp, k + 1)
                if k:
                    dve.wait_ge(coef_done, k)
                link(nc.vector.reciprocal(stat[:, 118:119], stat[:, 110 + k % 4:111 + k % 4]))
                dve.wait_ge(gelu_done, k + 1)
                if t:
                    dve.wait_ge(diag_done, H * TOPK * (t - 1) + (c + 1) * TOPK)
                nc.vector.scalar_tensor_tensor(coef[:, cols], gel[:, cols], stat[:, 118:119], soft[:, t % 2, cols],
                                               ALU.mult, ALU.mult)\
                    .then_inc(coef_done, 1)

            def finish(t):
                dve.wait_ge(acc_done, t + 1)
                if t:
                    dve.wait_ge(out_sent, 16 * t)
                nc.vector.tensor_tensor(ostage[:], x1[:, t, :], psum[:, 4 + 2 * (t % 2):6 + 2 * (t % 2), :]
                                        .rearrange("p a b -> p (a b)"), ALU.add).then_inc(acc_read, 1)

            dots(0, 0)
            for t in range(NT):
                for c in range(H):
                    if c == 1 and t:
                        finish(t - 1)
                    if c == NORM_AT and t + 1 < NT:
                        prep_norm(t + 1)
                    if H * t + c + AHEAD < CHUNKS:
                        prep_top(H * t + c + AHEAD)
                    if c + 1 < H:
                        dots(t, c + 1)
                    elif t + 1 < NT:
                        dots(t + 1, 0)
            weigh(NT - 1, H - 1)
            finish(NT - 1)

        @block.tensor
        def _(pe):
            def mm(o, l, r, start, stop):
                return nc.tensor.matmul(o, l, r, start=start, stop=stop)

            def finished(ins):
                ins.then_inc(dense_done, 1)

            pe.wait_ge(consts, 1)
            pe.wait_ge(xn_done, NT)
            for c in range(KC):
                wait_bank(pe, f"hT{c}")
                for t in range(NT):
                    last = nc.tensor.transpose(bank(f"hT{c}")[:, t * P:(t + 1) * P], xs[:, t, c * P:(c + 1) * P],
                                               ident[:])
                finished(last)
            pe.wait_ge(xn_done, NT + 1)
            wait_bank(pe, "hTm")
            for c in range(KC):
                last = nc.tensor.transpose(bank("hTm")[:, c * META:(c + 1) * META], xmeta[0:META, c * P:(c + 1) * P],
                                           ident[0:META, 0:META])
            finished(last)
            for tag in ("hT6", "hT7", "hTm"):
                wait_evac(pe, tag)

            def feature_major(name, meta=None):
                wait_weights(pe, name)
                w = weights(name)
                for c in range(CH):
                    tag = f"{name}{c}"
                    wait_bank(pe, tag)
                    for k in range(KC):
                        last = mm(bank(tag), w[:, k, c * P:(c + 1) * P], hT[:, k, META:L], k == 0, k == KC - 1)
                    finished(last)
                if meta:
                    wait_bank(pe, meta)
                    for c in range(CH):
                        for k in range(KC):
                            last = mm(bank(meta)[:, c * META:(c + 1) * META], w[:, k, c * P:(c + 1) * P],
                                      hT[:, k, 0:META], k == 0, k == KC - 1)
                    finished(last)

            feature_major("zp")
            feature_major("u", "um")
            feature_major("k", "km")
            pe.wait_ge(small_in, SMALL)
            wait_bank(pe, "f")
            for k in range(KC):
                last = mm(bank("f")[0:H, :], f_w[:, k, :], hT[:, k, META:L], k == 0, k == KC - 1)
            finished(last)
            wait_bank(pe, "fm")
            for k in range(KC):
                last = mm(bank("fm")[0:H, 0:META], f_w[:, k, :], hT[:, k, 0:META], k == 0, k == KC - 1)
            finished(last)
            feature_major("q")
            wait_weights(pe, "v")
            for t in range(NT):
                wait_bank(pe, f"v{t}")
                for k in range(KC):
                    last = mm(bank(f"v{t}"), hT[:, k, META + t * P:META + (t + 1) * P], weights("v")[:, k, :],
                              k == 0, k == KC - 1)
                finished(last)
            wait_bank(pe, "vm")
            for k in range(KC):
                last = mm(bank("vm")[0:META, :], hT[:, k, 0:META], weights("v")[:, k, :], k == 0, k == KC - 1)
            finished(last)
            for c in range(CH):
                pe.wait_ge(pooled, c + 1)
                wait_bank(pe, f"pm{c}")
                finished(mm(bank(f"pm{c}"), poolw[:, c, :], uT[:, c, META:L], True, True))
            feature_major("za")

            for by in "AV":
                pe.wait_ge(evac_sem[by], sum(b == by for _, b in plan[:before_attention]))
            pe.wait_ge(decay_done, 1)

            def scores1(n):
                i, h = ATT[n]
                if n >= 2:
                    pe.wait_ge(exp_done, n - 1)
                    if ATT[n - 2][0] == NT - 1:
                        pe.wait_ge(pT_copied, n - 1)
                b, lo = 2 * (n % 2), HD * (h % 2)
                q = qT[lo:lo + HD, h // 2, i * P:(i + 1) * P]
                w = (i + 1) * P
                mb, mc = (b, w) if i < NT - 1 else (b + 1, 0)
                for o, k0, k1 in ((psum[:, b, 0:w], META, META + w), (psum[:, mb, mc:mc + META], 0, META)):
                    mm(o, q, kT[lo:lo + HD, h // 2, k0:k1], True, False)
                    last = mm(o, sel8[:, h, :], negc[:, k0:k1], False, k0 == 0)
                    if k0:
                        last = mm(o[:, i * P:w], identb[:], masks[:, 0, :], False, True)
                last.then_inc(s_done, 1)

            def transposes1(n):
                i, h = ATT[n]
                pe.wait_ge(norm_done, n + 1)
                if n >= 2:
                    pe.wait_ge(pT_copied, n - 1)
                for j in range(i + 1):
                    nc.tensor.transpose(psum[:, 4 + n % 2, j * P:(j + 1) * P], Pb[:, n % 2, j * P:(j + 1) * P],
                                        ident[:])
                nc.tensor.transpose(meta_ps(n, i), Pb[:, n % 2, (i + 1) * P:(i + 1) * P + META], ident[:])\
                    .then_inc(pT_done, 1)

            def values1(n):
                i, h = ATT[n]
                pe.wait_ge(pT_copied, n + 1)
                if n % 2 == 0 and n:
                    pe.wait_ge(y_done, n // 2)
                o = psum[HD * (h % 2):HD * (h % 2) + HD, 6, 0:P]
                hc = slice(h * HD, (h + 1) * HD)
                mm(o, vmeta[0:META, hc], PT[0:META, n % 2, 4, :], True, False)
                for j in range(i + 1):
                    last = mm(o, vtok[:, j, hc], PT[:, n % 2, j, :], False, j == i)
                last.then_inc(pv_done, 1)

            scores1(0)
            for n in range(N1):
                if n + 1 < N1:
                    scores1(n + 1)
                s, c = GATES[n // 2]
                tag = f"g{s}{c}"
                name = f"g{s}{c // 4}"
                if n % 2 == 0:
                    wait_weights(pe, name)
                    wait_bank(pe, tag)
                for k in range(4 * (n % 2), 4 * (n % 2) + 4):
                    last = mm(bank(tag), weights(name)[:, k, (c % 4) * P:(c % 4 + 1) * P], hT[:, k, META:L], k == 0,
                              k == KC - 1)
                if n % 2:
                    finished(last)
                transposes1(n)
                if n:
                    values1(n - 1)
            values1(N1 - 1)

            pe.wait_ge(exp_done, N1)
            pe.wait_ge(pT_copied, N1)
            pe.wait_ge(y_done, N1 // 2)
            for c in range(KC):
                for s, (name, y) in enumerate((("wup0", zp), ("wup1", za))):
                    wait_weights(pe, name)
                    wait_bank(pe, f"up{s}{c}")
                    for k in range(CH):
                        last = mm(bank(f"up{s}{c}"), weights(name)[:, k, c * P:(c + 1) * P], y[:, k, :], k == 0,
                                  k == CH - 1)
                    finished(last)
            def transposed_rows(t):
                pe.wait_ge(xn_done, NT + 1 + t + 1)
                for j in range(2):
                    tag = f"x2T{t}{j}"
                    wait_bank(pe, tag)
                    for c in range(4):
                        last = nc.tensor.transpose(bank(tag)[:, c * P:(c + 1) * P],
                                                   xn2[:, t % 2, (4 * j + c) * P:(4 * j + c + 1) * P], ident[:])
                    finished(last)

            for t in range(NT):
                for e in range(2):
                    wait_bank(pe, f"y{t}{e}")
                    for k in range(KC):
                        pe.wait_ge(merged_done, k + 1)
                        wait_weights(pe, f"wout{k // 4}")
                        last = mm(bank(f"y{t}{e}"), gate[:, 0, k, t * P:(t + 1) * P],
                                  weights(f"wout{k // 4}")[:, k % 4, 512 * e:512 * e + 512], k == 0, k == KC - 1)
                    finished(last)
                if t:
                    transposed_rows(t - 1)
            transposed_rows(NT - 1)

            wait_evac(pe, "x2T31")
            for name in ("sq", "sk"):
                wait_weights(pe, name)
                for c in range(CH):
                    wait_bank(pe, f"{name}{c}")
                    for k in range(KC):
                        last = mm(bank(f"{name}{c}"), weights(name)[:, k, c * P:(c + 1) * P], x2T[:, k, :], k == 0,
                                  k == KC - 1)
                    finished(last)

            def token_major(tag, name, t, c0, c1):
                wait_weights(pe, name)
                wait_bank(pe, tag)
                for k in range(KC):
                    last = mm(bank(tag)[:, 0:c1 - c0], x2T[:, k, t * P:(t + 1) * P], weights(name)[:, k, c0:c1],
                              k == 0, k == KC - 1)
                finished(last)

            for t in range(NT):
                token_major(f"sv{t}", "sv", t, 0, 512)
            for t in range(NT):
                token_major(f"cq{t}", "cq", t, 0, CQ)
                token_major(f"ckv{t}", "ckv", t, 0, CKV + ROPE)
            def latents(t):
                pe.wait_ge(xn_done, 2 * NT + 1 + 2 * t + 2)
                for tag, n, c0 in ((f"cqT{t}", 3, 0), (f"ckvT{t}", 2, CQ)):
                    wait_bank(pe, tag)
                    for c in range(n):
                        last = nc.tensor.transpose(bank(tag)[:, c * P:(c + 1) * P],
                                                   cqt[:, t, c0 + c * P:c0 + (c + 1) * P], ident[:])
                    finished(last)
            latents(0)
            for t in range(NT):
                wait_evac(pe, f"ckvT{t}")
                for base, n, name, w in (("uq", 3, "uq", 4 * QK), ("ukv", 2, "ukv", 512)):
                    wait_weights(pe, name)
                    for j in range(2):
                        tag = f"{base}{t}{j}"
                        wait_bank(pe, tag)
                        for k in range(n):
                            last = mm(bank(tag)[:, 0:w], latT[:, 5 * (t % 2) + (k if n == 3 else 3 + k), :],
                                      weights(name)[:, k, j * w:(j + 1) * w], k == 0, k == n - 1)
                        finished(last)
                if t + 1 < NT:
                    latents(t + 1)
                for j in range(2):
                    pe.wait_ge(rope_done, 2 * t + j + 1)
                    for g in range(2):
                        tag = f"qkT{t}{j}{g}"
                        wait_bank(pe, tag)
                        for h in range(4):
                            last = nc.tensor.transpose(bank(tag)[0:QK, h * P:(h + 1) * P], rows[:, j, 4 * g + h, :],
                                                       ident[:])
                        finished(last)

            pe.wait_ge(act_evac, all_dense_a)
            pe.wait_ge(dve_evac, all_dense_v)

            def scores2(p):
                i, h = ATT[p]
                lo = HD * (h % 2)
                rows_keys = [(sq[lo:lo + HD, h // 2, i * P:(i + 1) * P], sk[lo:lo + HD, h // 2, 0:(i + 1) * P]),
                             (mq[0:QK, h, i * P:(i + 1) * P], mk[0:QK, h, 0:(i + 1) * P])]
                for kind in range(2):
                    if p >= 2:
                        pe.wait_ge((zr_done, exp2_done[1])[kind], p - 1)
                    o = psum[:, 2 * kind + p % 2, 0:(i + 1) * P]
                    mm(o, *rows_keys[kind], True, False)
                    mm(o[:, i * P:(i + 1) * P], identb[:], masks[:, 1 + kind, :], False, True)\
                        .then_inc(s2_done[kind], 1)

            def transposes2(p):
                i, h = ATT[p]
                for kind in (1, 0):
                    pe.wait_ge((exp2_done[0], ml_norm)[kind], p + 1)
                    if p:
                        pe.wait_ge(pT2_copied[kind], p)
                    for j in range(i + 1):
                        last = nc.tensor.transpose(psum[:, 4 + kind, j * P:(j + 1) * P],
                                                   Pb2[:, kind, j * P:(j + 1) * P], ident[:])
                    last.then_inc(pT2_done[kind], 1)

            def values2(p):
                i, h = ATT[p]
                if h % 2 == 0 and p:
                    pe.wait_ge(osq_done, p // 2)
                    pe.wait_ge(og_done, p)
                if h == 0 and i:
                    pe.wait_ge(oms_done, i)
                for kind in range(2):
                    pe.wait_ge(pT2_copied[kind], p + 1)
                    o = psum[HD * (h % 2):HD * (h % 2) + HD, 6, kind * P:(kind + 1) * P]
                    v = (sv, mv)[kind]
                    for j in range(i + 1):
                        last = mm(o, v[:, j, h * HD:(h + 1) * HD], PT2[:, kind, j, :], j == 0, j == i)
                last.then_inc(pv2_done, 1)

            def sums(q):
                pe.wait_ge(osq_done, q + 1)
                pe.wait_ge(og_done, 2 * q + 2)
                for kind in range(2):
                    at = 2 * P + CH * kind + q % CH
                    last = mm(psum[:, 6, at:at + 1], osq[:, q % 2, kind, :], ones[:], True, True)
                last.then_inc(oss_done, 1)

            def project(i, g):
                e, kind = divmod(g, 2)
                if i < NT - 1 and (i or g):
                    pe.wait_ge(x2_added, 4 * i + g)
                if i == NT - 1:
                    pe.wait_ge(x2_added, 4 * i)
                    pe.wait_ge(pT2_copied[0], N2)
                    pe.wait_ge(pT2_copied[1], N2)
                    pe.wait_ge(oms_done, NT)
                pe.wait_ge(og_done, 2 * CH * (i + 1))
                wait_weights(pe, f"wo{kind}")
                for k in range(CH):
                    last = mm(psum[:, wo_bank(i, g), :], og[:, CH * kind + k, i * P:(i + 1) * P],
                              weights(f"wo{kind}")[:, k, 512 * e:512 * e + 512], k == 0, k == CH - 1)
                last.then_inc(wo_done, 1)

            def prep_bank(n):
                if n >= 4:
                    pe.wait_ge(prep_evac, n - 3)
                else:
                    pe.wait_ge(zr_done, N2 - 1 + n // 2)
                    pe.wait_ge(exp2_done[1], N2 - 1 + n // 2)

            def prep_subk(j):
                wait_weights(pe, "subk")
                prep_bank(j)
                for c in range(4):
                    last = nc.tensor.transpose(prep_ps(j)[:, c * P:(c + 1) * P],
                                               weights("subk")[:, 4 * j + c, :], ident[:])
                last.then_inc(prep_mm, 1)

            scores2(0)
            scores2(1)
            for p, (i, h) in enumerate(ATT):
                if h % 2 == 1 and p >= 3:
                    sums((p - 3) // 2)
                if p:
                    values2(p - 1)
                if h in WO_AT and i:
                    project(i - 1, WO_AT.index(h))
                if p + 2 < N2:
                    scores2(p + 2)
                if p == N2 - 1:
                    prep_subk(0)
                    prep_subk(1)
                transposes2(p)
            prep_subk(2)
            prep_subk(3)
            values2(N2 - 1)

            def prepare(t, n):
                kind, j = PREP[n]
                g = SUBK_GROUPS + len(PREP) * t + n
                prep_bank(g)
                o = prep_ps(g)
                base = SUBK_GROUPS + len(PREP) * t
                if kind == "xT":
                    pe.wait_ge(p_xn, t + 1)
                    for c in range(4):
                        last = nc.tensor.transpose(o[:, c * P:(c + 1) * P],
                                                   xn[:, t % 2, (4 * j + c) * P:(4 * j + c + 1) * P], ident[:])
                elif kind == "q":
                    pe.wait_ge(prep_evac, base + 2)
                    wait_weights(pe, f"pq{j}")
                    for c in range(4):
                        for k in range(KC):
                            last = mm(o[:, c * P:(c + 1) * P], weights(f"pq{j}")[:, k, c * P:(c + 1) * P],
                                      xnT[:, k, :], k == 0, k == KC - 1)
                else:
                    pe.wait_ge(prep_evac, base + n)
                    for c in range(4):
                        h, half = divmod(4 * j + c, 2)
                        last = mm(o[:, c * P:(c + 1) * P], pq[:, 2 * h + half, :], skT[:, H * half + h, :], True, True)
                last.then_inc(prep_mm, 1)

            for n, (kind, j) in enumerate(PREP):
                prepare(0, n)
                if (kind, j) == ("xT", 1):
                    sums(N2 // 2 - 1)
                if (kind, j) == ("s", 0):
                    for g in range(4):
                        project(NT - 1, g)
            pe.wait_ge(x2_added, 4 * NT)

            def weighted(t, c):
                for s in range(c * TOPK, (c + 1) * TOPK):
                    g = v_gather(t, s)
                    n = H * TOPK * t + s
                    if s == 0 and t >= 2:
                        pe.wait_ge(acc_read, t - 1)
                    pe.wait_ge(diag_done, n + 1)
                    pe.wait_ge(landed[g % NB], 16 * (g // NB + 1))
                    for e in range(2):
                        last = mm(psum[:, 4 + 2 * (t % 2) + e, :], diag[:, n % 4, :], gathered[g % NB][:, 512 * e:512 * e + 512], s == 0,
                                  s == H * TOPK - 1)
                    last.then_inc(v_used, 1)
                    if s == H * TOPK - 1:
                        pe.wait_ge(v_used, n + 1)
                        pe.sem_inc(acc_done, 1)

            for t in range(NT):
                for c in range(H):
                    weighted(t, c)
                    if t + 1 < NT:
                        for n in PREP_AT[c]:
                            prepare(t + 1, n)



def kernel(**inputs):
    import numpy as _np
    import concourse.bacc as _bacc
    from concourse import mybir as _mybir
    from concourse.bass_utils import run_bass_kernel_spmd as _run

    nc = _bacc.Bacc("TRN2", target_bir_lowering=False, num_devices=1)
    arrays, aps = {}, {}
    for name, value in inputs.items():
        v = _np.ascontiguousarray(value)
        arrays[f"in_{name}"] = v
        aps[name] = nc.dram_tensor(f"in_{name}", v.shape, _mybir.dt.from_np(v.dtype), kind="ExternalInput").ap()
    out = nc.dram_tensor("out_0", (1, T, D), F32, kind="ExternalOutput").ap()
    build(nc, aps, out)
    return _run(nc, [arrays], core_ids=[0]).results[0]["out_0"]
```
